# Optimizing a Trainium2 kernel written in Bass

```python
import math
import jax, jax.numpy as jnp
from jax import lax
import numpy as np

"""Four-layer hybrid decoder trunk (Griffin-style parallel gated merge).

Each layer:
  h = RMSNorm(x)
  z = h @ W_in  -> [q | k | v (3 dilation groups x 8 heads x 64) | ssm input (512) | gate_attn (D) | gate_ssm (D)]
  A = dilated causal sliding-window attention (LongNet mixture of dilations, QK-norm, NoPE),
      groups combined per head slot by their softmax denominators, projected 512 -> D
  S = S5 complex-diagonal SSM (32 groups of 16 channels, 64 complex states each, ZOH),
      Re(C x) + D u, GELU, GLU whose two projections map 512 -> D
  x = x + (sigmoid(gate_attn) * A + sigmoid(gate_ssm) * S) @ W_out
  x = x + SwiGLU(RMSNorm(x))
Input x: (BATCH, SEQ, D_MODEL) float32; output: (BATCH, SEQ, D_MODEL).
"""

D_MODEL = 1024
BATCH = 1
SEQ = 512
DEPTH = 1

HEAD_DIM = 64
HEADS_PER_GROUP = D_MODEL // 2 // HEAD_DIM
ATTN_PATTERN = ((128, 1), (512, 4), (2048, 16))
N_ATTN_GROUPS = len(ATTN_PATTERN)
ATTN_WIDTH = HEADS_PER_GROUP * HEAD_DIM
QKV_GROUP_WIDTH = N_ATTN_GROUPS * ATTN_WIDTH
BLK = 128
SSM_WIDTH = D_MODEL // 2
SSM_GROUP = 16
SSM_GROUPS = SSM_WIDTH // SSM_GROUP
SSM_STATE = 64
DT_MIN = 1e-3
DT_MAX = 1e-1
D_FF = ((8 * D_MODEL + 3 * 256 - 1) // (3 * 256)) * 256
EPS = 1e-6
IN_COLS = 3 * QKV_GROUP_WIDTH + SSM_WIDTH + 2 * D_MODEL
SPLIT_POINTS = (QKV_GROUP_WIDTH, 2 * QKV_GROUP_WIDTH, 3 * QKV_GROUP_WIDTH,
                3 * QKV_GROUP_WIDTH + SSM_WIDTH, 3 * QKV_GROUP_WIDTH + SSM_WIDTH + D_MODEL)

kernel_name = "hybrid_gated_dilated_attn_s5_swiglu"

def rms_norm(t, gain):
    t32 = t.astype(jnp.float32)
    y = t32 * lax.rsqrt(jnp.mean(t32 * t32, axis=-1, keepdims=True) + EPS) * gain.astype(jnp.float32)
    return y.astype(t.dtype)

def head_rms_norm(t, gain):
    t32 = t.astype(jnp.float32)
    return t32 * lax.rsqrt(jnp.mean(t32 * t32, axis=-1, keepdims=True) + EPS) * gain.astype(jnp.float32)

def dilated_window_attention(q, k, v, window, dilation):
    b_, L, H, E = q.shape
    span = window // dilation
    unit = dilation * BLK
    Lp = -(-L // unit) * unit
    M = Lp // dilation
    nb = M // BLK

    def to_blocks(t):
        t = jnp.pad(t, ((0, 0), (0, Lp - L), (0, 0), (0, 0)))
        t = t.reshape(b_, M, dilation, H, E).transpose(0, 2, 3, 1, 4)
        return t.reshape(b_, dilation, H, nb, BLK, E)

    def with_prev(t):
        prev = jnp.pad(t[:, :, :, :-1], ((0, 0), (0, 0), (0, 0), (1, 0), (0, 0), (0, 0)))
        return jnp.concatenate([prev, t], axis=4)

    qb = to_blocks(q)
    kw = with_prev(to_blocks(k))
    vw = with_prev(to_blocks(v))
    s = jnp.einsum('brhnqe,brhnke->brhnqk', qb, kw) * (HEAD_DIM ** -0.5)
    qi = jnp.arange(BLK)[:, None]
    ki = jnp.arange(2 * BLK)[None, :]
    dist = BLK + qi - ki
    blk = jnp.arange(nb)[:, None, None]
    mask = (dist >= 0) & (dist <= span) & (blk * BLK + ki - BLK >= 0)
    s = jnp.where(mask, s, -jnp.inf)
    m = jnp.max(s, axis=-1, keepdims=True)
    p = jnp.exp(s - m)
    denom = jnp.sum(p, axis=-1, keepdims=True)
    o = jnp.einsum('brhnqk,brhnke->brhnqe', p, vw) / denom
    lse = (m + jnp.log(denom))[..., 0]
    o = o.reshape(b_, dilation, H, M, E).transpose(0, 3, 1, 2, 4).reshape(b_, Lp, H, E)[:, :L]
    lse = lse.reshape(b_, dilation, H, M).transpose(0, 3, 1, 2).reshape(b_, Lp, H)[:, :L]
    return o, lse

def dilated_attention(q, k, v, g_q, g_k):
    b_, L, _ = q.shape
    shape = (b_, L, N_ATTN_GROUPS, HEADS_PER_GROUP, HEAD_DIM)
    q = head_rms_norm(q.reshape(shape), g_q)
    k = head_rms_norm(k.reshape(shape), g_k)
    v = v.reshape(shape).astype(jnp.float32)
    outs, lses = [], []
    for gi, (window, dilation) in enumerate(ATTN_PATTERN):
        o, lse = dilated_window_attention(q[:, :, gi], k[:, :, gi], v[:, :, gi], window, dilation)
        outs.append(o)
        lses.append(lse)
    w = jax.nn.softmax(jnp.stack(lses, axis=0), axis=0)
    out = jnp.sum(w[..., None] * jnp.stack(outs, axis=0), axis=0)
    return out.reshape(b_, L, ATTN_WIDTH)

def _complex_linear_combine(e1, e2):
    a1r, a1i, b1r, b1i = e1
    a2r, a2i, b2r, b2i = e2
    ar = a2r * a1r - a2i * a1i
    ai = a2r * a1i + a2i * a1r
    br = a2r * b1r - a2i * b1i + b2r
    bi = a2r * b1i + a2i * b1r + b2i
    return (ar, ai, br, bi)

def s5_ssm(u, lam_re, lam_im, log_dt, b_re, b_im, c_re, c_im, d_skip):
    b_, L, _ = u.shape
    u = u.astype(jnp.float32)
    lr = lam_re.astype(jnp.float32)
    li = lam_im.astype(jnp.float32)
    dt = jnp.exp(log_dt.astype(jnp.float32))[:, None]
    mag = jnp.exp(lr * dt)
    ang = li * dt
    abar_re = mag * jnp.cos(ang)
    abar_im = mag * jnp.sin(ang)
    nr = abar_re - 1.0
    ni = abar_im
    den = lr * lr + li * li
    cr = ((nr * lr + ni * li) / den)[..., None]
    ci = ((ni * lr - nr * li) / den)[..., None]
    br = b_re.astype(jnp.float32)
    bi = b_im.astype(jnp.float32)
    bbar_re = cr * br - ci * bi
    bbar_im = cr * bi + ci * br
    ug = u.reshape(b_, L, SSM_GROUPS, SSM_GROUP)
    bu_re = jnp.einsum('blgc,gpc->lbgp', ug, bbar_re)
    bu_im = jnp.einsum('blgc,gpc->lbgp', ug, bbar_im)
    a_re = jnp.broadcast_to(abar_re[None, None], (L, 1, SSM_GROUPS, SSM_STATE))
    a_im = jnp.broadcast_to(abar_im[None, None], (L, 1, SSM_GROUPS, SSM_STATE))
    _, _, xr, xi = lax.associative_scan(_complex_linear_combine, (a_re, a_im, bu_re, bu_im), axis=0)
    y = (jnp.einsum('lbgp,gcp->blgc', xr, c_re.astype(jnp.float32))
         - jnp.einsum('lbgp,gcp->blgc', xi, c_im.astype(jnp.float32)))
    return y.reshape(b_, L, SSM_WIDTH) + d_skip.astype(jnp.float32) * u

def setup_inputs(seed: int = 0) -> dict:
    key = jax.random.key(seed)
    ks = jax.random.split(key, 24)
    f32 = jnp.float32

    def normal(k, shape, scale):
        return jax.random.normal(k, shape, f32) * scale

    n_idx = jnp.arange(SSM_STATE, dtype=f32)
    return {
        "x": normal(ks[0], (BATCH, SEQ, D_MODEL), 1.0),
        "g_mix": 1.0 + normal(ks[1], (DEPTH, D_MODEL), 0.02),
        "w_in": normal(ks[2], (DEPTH, D_MODEL, IN_COLS), D_MODEL ** -0.5),
        "g_q": 1.0 + normal(ks[3], (DEPTH, HEAD_DIM), 0.02),
        "g_k": 1.0 + normal(ks[4], (DEPTH, HEAD_DIM), 0.02),
        "w_attn_proj": normal(ks[5], (DEPTH, ATTN_WIDTH, D_MODEL), ATTN_WIDTH ** -0.5),
        "lambda_re": -0.5 + normal(ks[6], (DEPTH, SSM_GROUPS, SSM_STATE), 0.01),
        "lambda_im": math.pi * n_idx + normal(ks[7], (DEPTH, SSM_GROUPS, SSM_STATE), 0.01),
        "log_dt": jax.random.uniform(ks[8], (DEPTH, SSM_GROUPS), f32, math.log(DT_MIN), math.log(DT_MAX)),
        "b_re": normal(ks[9], (DEPTH, SSM_GROUPS, SSM_STATE, SSM_GROUP), (2 * SSM_GROUP) ** -0.5),
        "b_im": normal(ks[10], (DEPTH, SSM_GROUPS, SSM_STATE, SSM_GROUP), (2 * SSM_GROUP) ** -0.5),
        "c_re": normal(ks[11], (DEPTH, SSM_GROUPS, SSM_GROUP, SSM_STATE), (2 * SSM_STATE) ** -0.5),
        "c_im": normal(ks[12], (DEPTH, SSM_GROUPS, SSM_GROUP, SSM_STATE), (2 * SSM_STATE) ** -0.5),
        "d_skip": normal(ks[13], (DEPTH, SSM_WIDTH), 1.0),
        "w_glu_a": normal(ks[14], (DEPTH, SSM_WIDTH, D_MODEL), SSM_WIDTH ** -0.5),
        "w_glu_b": normal(ks[15], (DEPTH, SSM_WIDTH, D_MODEL), SSM_WIDTH ** -0.5),
        "w_out": normal(ks[16], (DEPTH, D_MODEL, D_MODEL), D_MODEL ** -0.5),
        "g_ffn": 1.0 + normal(ks[17], (DEPTH, D_MODEL), 0.02),
        "w_ffn_gate": normal(ks[18], (DEPTH, D_MODEL, D_FF), D_MODEL ** -0.5),
        "w_ffn_up": normal(ks[19], (DEPTH, D_MODEL, D_FF), D_MODEL ** -0.5),
        "w_ffn_down": normal(ks[20], (DEPTH, D_FF, D_MODEL), D_FF ** -0.5),
    }

def reference(x, g_mix, w_in, g_q, g_k, w_attn_proj, lambda_re, lambda_im, log_dt,
              b_re, b_im, c_re, c_im, d_skip, w_glu_a, w_glu_b, w_out,
              g_ffn, w_ffn_gate, w_ffn_up, w_ffn_down):
    for l in range(DEPTH):
        h = rms_norm(x, g_mix[l])
        z = h @ w_in[l]
        q, k, v, u, gate_a, gate_s = jnp.split(z, SPLIT_POINTS, axis=-1)
        a = dilated_attention(q, k, v, g_q[l], g_k[l]).astype(x.dtype)
        a_out = a @ w_attn_proj[l]
        y = s5_ssm(u, lambda_re[l], lambda_im[l], log_dt[l], b_re[l], b_im[l],
                   c_re[l], c_im[l], d_skip[l])
        y = jax.nn.gelu(y).astype(x.dtype)
        s_out = (y @ w_glu_a[l]) * jax.nn.sigmoid(y @ w_glu_b[l])
        mix = jax.nn.sigmoid(gate_a) * a_out + jax.nn.sigmoid(gate_s) * s_out
        x = x + mix @ w_out[l]
        h2 = rms_norm(x, g_ffn[l])
        x = x + (jax.nn.silu(h2 @ w_ffn_gate[l]) * (h2 @ w_ffn_up[l])) @ w_ffn_down[l]
    return x


_drawn_inputs = setup_inputs


def setup_inputs(seed=0):
    import zlib

    import numpy as np

    out = dict(_drawn_inputs(seed))
    spreads = {}
    factors = {'g_mix': 8.0,
     'g_q': 8.0,
     'g_k': 8.0,
     'lambda_re': 64.0,
     'lambda_im': 39.088,
     'log_dt': 39.408,
     'b_re': 55.128,
     'b_im': 56.256,
     'c_re': 55.448,
     'c_im': 55.392,
     'g_ffn': 3.942}
    for name, (base, spread) in spreads.items():
        noise = np.random.default_rng([zlib.crc32(name.encode()), seed]).standard_normal(out[name].shape)
        drawn = base * np.exp(spread * noise) if base else spread * noise
        out[name] = __import__('jax').numpy.asarray(drawn.astype(out[name].dtype))
    for name, factor in factors.items():
        out[name] = (out[name] * factor).astype(out[name].dtype)
    return out
```

```python
from contextlib import ExitStack

import numpy as np

import concourse.bass as bass
from concourse import mybir

F32 = mybir.dt.float32
F32R = mybir.dt.float32r
ALU = mybir.AluOpType
ACT = mybir.ActivationFunctionType
AX_X = mybir.AxisListType.X

P = 128
SEQ = 512
DM = 1024
TB = SEQ // P
KT = DM // P
HD = 64
NPAIR = 4
AW = 512
FF = 2816
FT = FF // P
FB = FF // 256
EPS = 1e-6
NG = 32
NPR = NG // 2
CH = 16
CL = 8
NC = SEQ // CL
WRAW = 4
WSPL = 2
OW = HD + 2

W_U = 0
W_V = W_U + 4
W_QK = W_V + 12
W_GATE = W_QK + 24
W_MIX = W_GATE + 16
W_OUT = W_MIX + 12
W_FFN = W_OUT + 8
W_DOWN = W_FFN + 4 * FB
W_END = W_DOWN + FT

TWO_PI = 6.283185307179586
C1 = 6.28125
C2 = 0.0019350051879882812
C3 = TWO_PI - C1 - C2
ROUND = 12582912.0
PI_BELOW = 3.1415925
NEG = -1.0e30


N_PARAMS = 23
PARAMS = 16 * N_PARAMS


def build(nc, t):
    with ExitStack() as ctx:
        sems = {}

        def sem(name):
            if name not in sems:
                sems[name] = ctx.enter_context(nc.semaphore(name))
            return sems[name]

        def sb(stack, name, shape, dt=F32):
            return stack.enter_context(nc.sbuf_tensor(name, shape, dt))

        hT_hi = sb(ctx, "hT_hi", [P, KT, SEQ], F32R)
        hT_lo = sb(ctx, "hT_lo", [P, KT, SEQ], F32R)
        w_raw = sb(ctx, "w_raw", [P, WRAW, 1024])
        w_hi = sb(ctx, "w_hi", [P, WSPL, 1024], F32R)
        w_lo = sb(ctx, "w_lo", [P, WSPL, 1024], F32R)
        masks = sb(ctx, "masks", [P, 4 * P])
        ident = sb(ctx, "ident", [P, P])
        eye16 = sb(ctx, "eye16", [P, CH])
        gmixT = sb(ctx, "gmixT", [P, KT])
        gffnT = sb(ctx, "gffnT", [P, KT])
        gqk = sb(ctx, "gqk", [P, 3])
        row_ss = sb(ctx, "row_ss", [P, TB])
        row_r = sb(ctx, "row_r", [P, TB])
        minus_half = sb(ctx, "minus_half", [P, 32])


        with nc.sbuf_tensor("early", [P, 34816], F32) as early:
            pass
        at = [0]

        def cut(arena, n, at=at):
            at[0] += n
            return arena[:, at[0] - n:at[0]]

        x_in_f = cut(early, TB * DM)
        zs = cut(early, 2 * TB * AW).rearrange("p (b m c) -> p b m c", b=2, m=TB)
        zsq = cut(early, 2304)
        aB_f = cut(early, 2 * NPR * CL * CH)
        ca = cut(early, 2 * NPR * (CL + 1) * CH).rearrange("p (r q k c) -> p r q k c", r=2, q=NPR, k=CL + 1)
        toep_f = cut(early, NG * CL * CH)
        rot_f = cut(early, 2 * NPR * NC)
        uc_f = cut(early, NG * NC)
        m8row_f = cut(early, NPR * NC)
        bb_f = cut(early, 2 * (NPR + 1) * CH)
        cnat = cut(early, 2 * 2 * P).rearrange("p (r h x) -> p r h x", r=2, h=2)
        ctr_f = cut(early, 2 * NPR * CH)
        bnat = cut(early, 2 * NPR * CH).rearrange("p (r q c) -> p r q c", r=2, q=NPR)
        kall_f = cut(early, 1024)
        xst = cut(early, 2 * NPR * (NC + 1)).rearrange("p (r q c) -> p r q c", r=2, q=NPR)
        dsk = cut(early, 8)
        dadd = cut(early, 8 * CH).rearrange("p (g c) -> p g c", g=8)
        states = cut(early, 24 * NPR).rearrange("p (n q) -> p n q", n=24)
        apw = cut(early, 2 * (CL + 1) * NPR).rearrange("p (r k q) -> p r k q", r=2, k=CL + 1)
        apn = cut(early, (CL + 1) * NPR).rearrange("p (k q) -> p k q", k=CL + 1)
        z_ss = cut(early, 32)
        z_r = cut(early, 32)
        x_in = x_in_f.rearrange("p (n c) -> p n c", n=TB)
        uT = x_in_f[:, 0:4 * SEQ].rearrange("p (m x) -> p m x", m=4)
        w1T = x_in_f.rearrange("p (r q x) -> p r q x", r=2, q=NPR)
        aB = aB_f.rearrange("p (r q k c) -> p r q k c", r=2, q=NPR, k=CL)
        toep = toep_f.rearrange("p (g x) -> p g x", g=NG)
        rot = rot_f.rearrange("p (r q c) -> p r q c", r=2, q=NPR)
        uc = uc_f.rearrange("p (g c) -> p g c", g=NG)
        m8row = m8row_f.rearrange("p (q c) -> p q c", q=NPR)
        ctr = ctr_f.rearrange("p (r q c) -> p r q c", r=2, q=NPR)
        bb = bb_f.rearrange("p (r q c) -> p r q c", r=2, q=NPR + 1)
        kall = kall_f.rearrange("p (h q x) -> p h q x", h=2, q=4)
        turned = [aB_f[:, n * 1024:(n + 1) * 1024] for n in range(4)]
        ygelu = rot_f.rearrange("p (q h c) -> p h q c", q=NPR, h=2)
        LR, LI, DT, ZR, ANG, KQ, RR, DEN, SQ, RD, MAG, M8, SIN, S2, COS, NR, T1, T2, CR, CI, ER, EI, FR, FI = range(24)
        sv = [states[:, n, :] for n in range(24)]

        late_stack = ExitStack()
        yT_hi = sb(late_stack, "yT_hi", [P, 4, SEQ], F32R)
        yT_lo = sb(late_stack, "yT_lo", [P, 4, SEQ], F32R)
        aT_hi = sb(late_stack, "aT_hi", [P, 4, SEQ], F32R)
        aT_lo = sb(late_stack, "aT_lo", [P, 4, SEQ], F32R)
        late = sb(late_stack, "late", [P, 26624])
        late_stack.close()
        off = lambda a, n: late[:, a:a + n]
        zt = off(0, 3072).rearrange("p (s n c) -> p s n c", s=6, n=TB)
        V_AT, V_STEP = 3072, 12544
        vt = [off(V_AT + b * V_STEP, 1536).rearrange("p (g n c) -> p g n c", g=3, n=TB) for b in range(2)]
        qT = off(4608, 1536).rearrange("p (g t) -> p g t", g=3)
        kT = off(6144, 1536).rearrange("p (g t) -> p g t", g=3)
        negs = off(7680, 1024).rearrange("p (b k) -> p b k", b=2)
        prob = off(8704, 1024).rearrange("p (b k) -> p b k", b=2)
        probT = off(9728, 1024).rearrange("p (b k) -> p b k", b=2)
        ost = [off(a, 1056).rearrange("p (s n h e) -> p s n h e", s=2, n=TB, h=2) for a in (10752, 25344)]
        yT_raw = off(11808, 2048).rearrange("p (m x) -> p m x", m=4)
        gate = off(17152, 8192).rearrange("p (m t) -> p m t", m=16)
        oall = off(0, 4224).rearrange("p (s n g e) -> p s n g e", s=2, n=TB, g=8)
        oall_d = off(0, 4224).rearrange("p (s n i x) -> p s n i x", s=2, n=TB, i=NPAIR)
        a_tok = off(4608, 2048).rearrange("p (n g e) -> p n g e", n=TB, g=8)
        a_tmp = off(7680, 2048).rearrange("p (n g e) -> p n g e", n=TB, g=8)
        cmb = off(9728, 5 * 2 * 32).rearrange("p (x s n g) -> p x s n g", x=5, s=2, n=TB)
        sgb = off(13856, 2048).rearrange("p (m t) -> p m t", m=4)
        x1 = off(0, 4096).rearrange("p (n c) -> p n c", n=TB)
        xn2 = off(4096, 4096).rearrange("p (n c) -> p n c", n=TB)
        s_raw = off(8192, FT * SEQ).rearrange("p (m t) -> p m t", m=FT)
        sg = off(19456, 1024).rearrange("p (m t) -> p m t", m=2)
        oT = off(20480, 4096).rearrange("p (m t) -> p m t", m=KT)
        y_out = off(4096, 4096).rearrange("p (n c) -> p n c", n=TB)

        ps = ctx.enter_context(nc.psum_tensor("ps", [P, 8, 512], F32))

        z_d = nc.dram_tensor("z_d", (9, SEQ, AW), F32, kind="Internal").ap()
        u_d = nc.dram_tensor("u_d", (NG * CH, CL, NC), F32, kind="Internal").ap()
        k_d = nc.dram_tensor("k_d", (NG, CH, CL * CH), F32, kind="Internal").ap()
        y_d = nc.dram_tensor("y_d", (NG * CH, CL, NC), F32, kind="Internal").ap()
        o_d = nc.dram_tensor("o_d", (2, NPAIR, SEQ, 2 * OW), F32, kind="Internal").ap()

        raw_landed = [sem(f"raw_landed{s}") for s in range(WRAW)]
        w_hi_done, w_lo_done = sem("w_hi_done"), sem("w_lo_done")
        gemm_steps = sem("gemm_steps")
        act_evac, dve_evac = sem("act_evac"), sem("dve_evac")
        misc_act, misc_dve = sem("misc_act"), sem("misc_dve")
        x_loaded, params_in, dsk_in = sem("x_loaded"), sem("params_in"), sem("dsk_in")
        act_tab, dve_tab, pool_tab = sem("act_tab"), sem("dve_tab"), sem("pool_tab")
        sumsq_done, row_r_done, xn_done = sem("sumsq_done"), sem("row_r_done"), sem("xn_done")
        x_turned, hT_hi_done, hT_lo_done = sem("x_turned"), sem("hT_hi_done"), sem("hT_lo_done")
        c_turned = sem("c_turned")
        u_stored, uc_loaded = sem("u_stored"), sem("uc_loaded")
        z_stored, z_sq, z_sum, z_scaled, z_pool = sem("z_stored"), sem("z_sq"), sem("z_sum"), sem("z_scaled"), sem("z_pool")
        w1_filled, kall_done, kall_out = sem("w1_filled"), sem("kall_done"), sem("kall_out")
        k_stored, toep_in = sem("k_stored"), sem("toep_in")
        s_done, scan_step, xst_done, y_done = sem("s_done"), sem("scan_step"), sem("xst_done"), sem("y_done")
        y_stored, yT_hi_done, yT_lo_done = sem("y_stored"), sem("yT_hi_done"), sem("yT_lo_done")
        zt_qk_in, zt_v_in = sem("zt_qk_in"), sem("zt_v_in")
        qk_turned, scores_done, prob_done, prob_turned, o_done = (
            sem("qk_turned"), sem("scores_done"), sem("prob_done"), sem("prob_turned"), sem("o_done"))
        o_stored, oall_in = [sem(f"o_stored{b}") for b in range(2)], sem("oall_in")
        cmb_dve, cmb_act, a_ready, a_turned, aT_hi_done, aT_lo_done = (
            sem("cmb_dve"), sem("cmb_act"), sem("a_ready"), sem("a_turned"), sem("aT_hi_done"), sem("aT_lo_done"))
        glu_done, mix_mul, mix_done, mix_hi_done, mix_lo_done = (
            sem("glu_done"), sem("mix_mul"), sem("mix_done"), sem("mix_hi_done"), sem("mix_lo_done"))
        x1_in = sem("x1_in")
        s_done2, s_hi_done, s_lo_done = sem("mid_done"), sem("mid_hi_done"), sem("mid_lo_done")
        down_done, down_evac, out_turned, out_done, out_stored = (
            sem("down_done"), sem("down_evac"), sem("out_turned"), sem("out_done"), sem("out_stored"))

        O_FREE = 16
        MA_C, MA_W1, MA_K, MA_Y = 2, 6, 8, 12
        MD_W1, MD_S = 4, 5
        MA_PAIR, MD_PAIR = 11, 19
        MA_ATT, MD_ATT = MA_Y + NPAIR * MA_PAIR, MD_S + NPAIR * MD_PAIR

        def ma_probT(u):
            return 3 + u + 1

        def md_scores(u):
            return 3 + u + 1 + max(0, u - 2)

        def md_out(u):
            return 3 + min(8, u + 3) + u + 1

        AE_U, DE_U = 2, 2
        AE_Z, DE_Z = AE_U + 18, DE_U + 18
        AE_G = AE_Z + 16
        AE_GLU, DE_GLU = AE_G + 8, DE_Z + 8
        DE_MIX = DE_GLU + 8
        DE_OUT = DE_MIX + 8
        AE_F, DE_F = AE_GLU + 2 * FB, DE_OUT + 2 * FB

        def wait_apart(eng, *waits):
            values = [eng.to_reg(value) for _, value in waits]
            eng.wait_ge(params_in, PARAMS)
            for (s, _), value in zip(waits, values):
                eng.wait_ge(s, value)

        TAB = {}
        ctx.enter_context(nc.allow_non_contiguous_dma(reason="small parameters"))
        block = ctx.enter_context(nc.Block())

        def in_cols(cc):
            return lambda j, h: t["w_in"][bass.ds((2 * j + h) * P, P), bass.ds(cc * 512, 512)]

        def cols(w, c):
            return lambda j, h: w[(2 * j + h) * P:(2 * j + h + 1) * P, c * 512:(c + 1) * 512]

        @block.sync
        def _(sp):
            def load(w, j, src, slot=None):
                if not (isinstance(w, int) and w < WRAW):
                    sp.wait_ge(w_lo_done, w - WRAW + 1)
                for h in range(2):
                    sp.dma_start(w_raw[:, j % WRAW, h * 512:(h + 1) * 512], src(j, h)).then_inc(raw_landed[j % WRAW], 16)

            def store_z(sec, par):
                sp.dma_start(z_d[bass.ds(sec, 1)].rearrange("s (m p) c -> p (s m) c", p=P),
                             zs[:, bass.ds(par, 1)].rearrange("p b m c -> p (b m) c")).then_inc(z_stored, 16)

            sp.dma_start(x_in, t["x"].rearrange("b (n p) c -> p (b n) c", p=P)).then_inc(x_loaded, 16)
            for j in range(4):
                load(W_U + j, j, in_cols(9))
            for j in range(4):
                load(W_V + j, j, in_cols(6))
            sp.wait_ge(act_evac, AE_U)
            sp.wait_ge(dve_evac, DE_U)
            sp.dma_start(u_d.rearrange("(m p) j c -> p m (j c)", p=P), uT).then_inc(u_stored, 16)
            sp.wait_ge(u_stored, 16)
            ug = u_d.rearrange("(g h) j c -> h g j c", h=CH)
            for j in range(CL):
                sp.dma_start(uc[(CL - 1 - j) * CH:(CL - j) * CH], ug[:, :, j, :]).then_inc(uc_loaded, 16)
            with sp.Fori(1, 3) as c:
                for j in range(4):
                    load(W_V + 4 * c + j, j, in_cols(c + 6))
                sp.wait_ge(act_evac, AE_U + 2 * c)
                sp.wait_ge(dve_evac, DE_U + 2 * c)
                store_z(c + 5, (c + 1) % 2)
                wait_apart(sp, (z_stored, 16 * c))
            for j in range(4):
                load(W_QK + j, j, in_cols(0))
            sp.wait_ge(act_evac, AE_U + 6)
            sp.wait_ge(dve_evac, DE_U + 6)
            store_z(8, 0)
            sp.wait_ge(z_stored, 48)
            with sp.Fori(1, 6) as c:
                for j in range(4):
                    load(W_QK + 4 * c + j, j, in_cols(c))
                sp.wait_ge(z_scaled, c)
                store_z(c - 1, c % 2)
                wait_apart(sp, (z_stored, 16 * c + 48))
            for j in range(4):
                load(W_GATE + j, j, in_cols(10))
            sp.wait_ge(z_scaled, 6)
            store_z(5, 0)
            sp.wait_ge(z_stored, 16 * 9)

            def load_rows(sec, dst, i, done):
                src = z_d[sec][:, bass.ds(i * P, P)]
                if sec % 3 == 0:
                    sp.dma_start(dst.rearrange("p (n c) -> p n c", n=TB), src.rearrange("(n p) c -> p n c", p=P)
                                 ).then_inc(done, 16)
                else:
                    v = src.rearrange("(m a b) c -> a m b c", a=4, b=4)
                    for b in range(4):
                        sp.dma_start(dst[:, b * P:(b + 1) * P], v[:, :, b]).then_inc(done, 16)

            def load_pair(i):
                for s in range(6):
                    load_rows(s, off(s * 512, 512), i, zt_qk_in)

            def load_values(i):
                for g in range(3):
                    load_rows(6 + g, late[:, bass.ds((i % 2) * V_STEP + (V_AT + g * 512), 512)], i, zt_v_in)

            load_pair(0)
            load_values(0)
            for b in range(2):
                sp.wait_ge(o_stored[b], O_FREE)
            with sp.Fori(1, NPAIR) as i:
                sp.wait_ge(qk_turned, 6 * i)
                load_pair(i)
                sp.wait_ge(o_done, 8 * i - 7)
                load_values(i)
                for j in range(4):
                    load(W_GATE + 4 * i + j, j, in_cols(i + 10))
            w = W_MIX
            for mat, c in (("b", 0), ("a", 0), ("b", 1), ("a", 1), ("p", 0), ("p", 1)):
                src = t[{"b": "w_glu_b", "a": "w_glu_a", "p": "w_attn_proj"}[mat]]
                for j in range(2):
                    sp.wait_ge(w_lo_done, w - WRAW + 1)
                    for h in range(2):
                        sp.dma_start(w_raw[:, w % WRAW, h * 512:(h + 1) * 512],
                                     cols(src, c)(j, h)).then_inc(raw_landed[w % WRAW], 16)
                    w += 1
            for c in range(2):
                for j in range(4):
                    load(W_OUT + 4 * c + j, j, cols(t["w_out"], c))
                if c == 0:
                    sp.wait_ge(a_ready, 1)
                    sp.dma_start(x1, t["x"].rearrange("b (n p) c -> p (b n) c", p=P)).then_inc(x1_in, 16)
            with sp.Fori(0, FB) as f:
                for j in range(4):
                    sp.wait_ge(w_lo_done, W_FFN - WRAW + 1 + j + 4 * f)
                    for h, name in enumerate(("w_ffn_gate", "w_ffn_up")):
                        sp.dma_start(w_raw[:, j, h * 512:(h + 1) * 512].rearrange("p (k c) -> p k c", k=2),
                                     t[name][2 * j * P:(2 * j + 2) * P, bass.ds(f * 256, 256)]
                                     .rearrange("(k p) c -> p k c", p=P)).then_inc(raw_landed[j], 16)

            def down(w, j, row):
                sp.wait_ge(w_lo_done, w - WRAW + 1)
                for h in range(2):
                    sp.dma_start(w_raw[:, j, h * 512:(h + 1) * 512],
                                 t["w_ffn_down"][bass.ds(row * P, P), h * 512:(h + 1) * 512]).then_inc(raw_landed[j], 16)

            with sp.Fori(0, FT // 4) as q:
                for j in range(4):
                    down(W_DOWN + j + 4 * q, j, q * 4 + j)
            for j in range(FT % 4):
                down(W_DOWN + FT // 4 * 4 + j, j, FT // 4 * 4 + j)
            for h in range(2):
                sp.wait_ge(out_done, 4 * (h + 1))
                sp.dma_start(t["out"].rearrange("b (n p) c -> p (b n) c", p=P)[:, :, h * 512:(h + 1) * 512],
                             y_out[:, :, h * 512:(h + 1) * 512]).then_inc(out_stored, 16)
            sp.wait_ge(out_stored, 32)

        @block.gpsimd
        def _(pool):
            n_tab = [0]

            def tab(ins):
                n_tab[0] += 1
                ins.then_inc(pool_tab, 1)
                pool.wait_ge(pool_tab, n_tab[0])

            def tt(out, a, b, op):
                tab(pool.tensor_tensor(out, a, b, op))

            def cmul(out_r, out_i, ar, ai, br, bi, tmp):
                tt(out_r, ar, br, ALU.mult)
                tt(tmp, ai, bi, ALU.mult)
                tt(out_r, out_r, tmp, ALU.subtract)
                tt(out_i, ar, bi, ALU.mult)
                tt(tmp, ai, br, ALU.mult)
                tt(out_i, out_i, tmp, ALU.add)

            tab(pool.memset(minus_half[:, :], -0.5))
            tab(pool.memset(dsk, 0.0))
            d4 = t["d_skip"].rearrange("o (r q h c) -> q c h (o r)", r=4, q=4, h=2)
            for q in range(4):
                for h in range(2):
                    pool.dma_start(dsk[32 * q:32 * q + CH, 4 * h:4 * h + 4], d4[q, :, h, :]).then_inc(dsk_in, 16)
            pool.wait_ge(sumsq_done, TB)
            tab(pool.tensor_scalar(row_ss[:, :], row_ss[:, :], 1.0 / DM, EPS, ALU.mult, ALU.add))
            pool.tensor_tensor(row_r[:, :], row_ss[:, :], minus_half[:, 0:TB], ALU.pow).then_inc(row_r_done, 1)
            tab(pool.memset(toep_f, 0.0))
            tab(pool.memset(bb_f, 0.0))
            pool.wait_ge(act_tab, 5)
            pool.wait_ge(dve_tab, 14)
            pool.wait_ge(params_in, PARAMS)
            tt(sv[COS], sv[S2], sv[S2], ALU.mult)
            tab(pool.tensor_scalar(sv[COS], sv[COS], -2.0, 1.0, ALU.mult, ALU.add))
            tab(pool.memset(apw[:, 0, 0, :], 1.0))
            tab(pool.memset(apw[:, 1, 0, :], 0.0))
            tt(apw[:, 0, 1, :], sv[MAG], sv[COS], ALU.mult)
            tt(apw[:, 1, 1, :], sv[MAG], sv[SIN], ALU.mult)
            tab(pool.tensor_scalar(sv[NR], apw[:, 0, 1, :], -1.0, None, ALU.add))
            tt(sv[T1], sv[NR], sv[LR], ALU.mult)
            tt(sv[T2], apw[:, 1, 1, :], sv[LI], ALU.mult)
            tt(sv[T1], sv[T1], sv[T2], ALU.add)
            tt(sv[CR], sv[T1], sv[RD], ALU.mult)
            tt(sv[T1], apw[:, 1, 1, :], sv[LR], ALU.mult)
            tt(sv[T2], sv[NR], sv[LI], ALU.mult)
            tt(sv[T1], sv[T1], sv[T2], ALU.subtract)
            tt(sv[CI], sv[T1], sv[RD], ALU.mult)
            over_ch = lambda a: a.unsqueeze(2).to_broadcast([P, NPR, CH])
            cmul(bb[:, 0, 0:NPR, :], bb[:, 1, 0:NPR, :], bnat[:, 0], bnat[:, 1], over_ch(sv[CR]), over_ch(sv[CI]),
                 zsq[:, 0:NPR * CH].rearrange("p (q c) -> p q c", q=NPR))
            for k, n in ((1, 1), (2, 2), (4, 4)):
                at_k = lambda r: apw[:, r, k:k + 1, :].to_broadcast([P, n, NPR])
                cmul(apw[:, 0, k + 1:k + 1 + n, :], apw[:, 1, k + 1:k + 1 + n, :],
                     apw[:, 0, 1:1 + n, :], apw[:, 1, 1:1 + n, :], at_k(0), at_k(1),
                     zsq[:, 0:n * NPR].rearrange("p (k q) -> p k q", k=n))
            tab(pool.tensor_scalar(apn, apw[:, 1], -1.0, None, ALU.mult))
            for_k = lambda a, n: a[:, 0:n, :].rearrange("p k q -> p q k").unsqueeze(3).to_broadcast([P, NPR, n, CH])
            for_c = lambda a, n: a.unsqueeze(2).to_broadcast([P, NPR, n, CH])
            tmp = lambda n: zsq[:, 0:NPR * n * CH].rearrange("p (q k c) -> p q k c", q=NPR, k=n)
            cmul(aB[:, 0], aB[:, 1], for_k(apw[:, 0], CL), for_k(apw[:, 1], CL),
                 for_c(bb[:, 0, 0:NPR], CL), for_c(bb[:, 1, 0:NPR], CL), tmp(CL))
            pool.wait_ge(misc_act, MA_C)
            cmul(ca[:, 0], ca[:, 1], for_k(apw[:, 0], CL + 1), for_k(apn, CL + 1),
                 for_c(ctr[:, 0], CL + 1), for_c(ctr[:, 1], CL + 1), tmp(CL + 1))
            TAB["ca"] = n_tab[0]
            small = sv[T1]
            cmul(sv[ER], sv[EI], sv[COS], sv[SIN], sv[COS], sv[SIN], small)
            cmul(sv[FR], sv[FI], sv[ER], sv[EI], sv[ER], sv[EI], small)
            cmul(sv[ER], sv[EI], sv[FR], sv[FI], sv[FR], sv[FI], small)
            tab(pool.memset(rot[:, 0, :, 0:1], 1.0))
            tab(pool.memset(rot[:, 1, :, 0:1], 0.0))
            n = 1
            while n < NC:
                by = lambda a: a.unsqueeze(2).to_broadcast([P, NPR, n])
                cmul(rot[:, 0, :, n:2 * n], rot[:, 1, :, n:2 * n], rot[:, 0, :, 0:n], rot[:, 1, :, 0:n],
                     by(sv[ER]), by(sv[EI]), zsq[:, 0:NPR * n].rearrange("p (q c) -> p q c", q=NPR))
                cmul(sv[FR], sv[FI], sv[ER], sv[EI], sv[ER], sv[EI], small)
                tab(pool.tensor_copy(sv[ER], sv[FR]))
                tab(pool.tensor_copy(sv[EI], sv[FI]))
                n *= 2
            tab(pool.tensor_copy(m8row, sv[M8].unsqueeze(2).to_broadcast([P, NPR, NC])))
            tab(pool.memset(m8row[:, :, 0:1], 0.0))
            tab(pool.memset(xst[:, :, :, 0:1], 0.0))
            TAB["all"] = n_tab[0]

            pool.wait_ge(kall_out, 2)
            for q in range(4):
                for h in range(2):
                    pool.dma_start(k_d.rearrange("(r q h) c x -> q h c r x", r=4, q=4)[q, h],
                                   kall[32 * q:32 * q + CH, h]).then_inc(k_stored, 16)
            pool.wait_ge(k_stored, 128)
            kg = k_d.rearrange("g c x -> c g x")
            for j in range(CL):
                n = (j + 1) * CH
                pool.dma_start(toep[j * CH:(j + 1) * CH, :, CL * CH - n:CL * CH], kg[:, :, 0:n]).then_inc(toep_in, 16)

            with pool.Fori(0, 6) as c:
                pool.wait_ge(act_evac, AE_U + 8 + 2 * c)
                pool.wait_ge(dve_evac, DE_U + 8 + 2 * c)
                zc = zs[:, bass.ds((c + 1) % 2, 1)].rearrange("p b m c -> p (b m c)")
                pool.tensor_tensor(zsq[:, 0:2048], zc, zc, ALU.mult).then_inc(z_sq, 1)
                wait_apart(pool, (z_sum, c + 1))
                pool.tensor_scalar(z_r, z_ss, 1.0 / HD, EPS, ALU.mult, ALU.add).then_inc(z_pool, 1)
                pool.wait_ge(z_pool, 2 * c + 1)
                pool.tensor_tensor(z_r, z_r, minus_half[:, :], ALU.pow).then_inc(z_pool, 1)
                wait_apart(pool, (z_pool, 2 * c + 2))
                zh = zc.rearrange("p (g e) -> p g e", e=HD)
                pool.tensor_tensor(zh, zh, z_r.unsqueeze(2).to_broadcast([P, 32, HD]), ALU.mult).then_inc(z_scaled, 1)

            def store_o(i, b):
                dst = o_d[0][bass.ds(i, 1)].rearrange("i (n p) x -> p (i n) x", p=P)
                pool.dma_start(dst, ost[b][:, 0].rearrange("p n h e -> p n (h e)")).then_inc(o_stored[b], 16)
                dst = o_d[1][bass.ds(i, 1)].rearrange("i (m a b) x -> (i a) m b x", a=4, b=4)
                src = ost[b][:, 1].rearrange("p n h e -> p n (h e)")
                for c in range(4):
                    pool.dma_start(dst[:, :, c], src[:, c]).then_inc(o_stored[b], 16)

            pool.wait_ge(misc_act, MA_Y)
            for i in range(CL):
                pool.dma_start(y_d.rearrange("(q h c) i k -> i c q h k", q=NPR, h=2)[i],
                               rot_f.rearrange("p (q h c) -> p q h c", q=NPR, h=2)[i * CH:(i + 1) * CH]).then_inc(y_stored, 16)
            pool.wait_ge(y_stored, 16 * CL)
            for b in range(2):
                pool.dma_start(yT_raw[:, 2 * b:2 * b + 2], y_d.rearrange("(m p) i k -> p m (i k)", p=P)[:, 2 * b:2 * b + 2]
                               ).then_inc(o_stored[b], O_FREE)
            with pool.Fori(0, NPAIR // 2) as i2:
                for b in range(2):
                    i = i2 * 2 + b
                    pool.wait_ge(misc_dve, MD_S + MD_PAIR + MD_PAIR * i)
                    store_o(i, b)
            for b in range(2):
                pool.wait_ge(o_stored[b], O_FREE + 80 * NPAIR // 2)
            for s in range(2):
                for n in range(TB):
                    pool.dma_start(oall_d[:, s, n], o_d[s][:, n * P:(n + 1) * P, :].rearrange("i p x -> p i x")
                                   ).then_inc(oall_in, 16)
            for c in range(2):
                for m in range(4):
                    pool.wait_ge(dve_evac, DE_Z + 4 * c + m + 1)
                    g = gate[:, 8 + 4 * c + m]
                    pool.tensor_tensor(g, g, sgb[:, m], ALU.mult).then_inc(glu_done, 1)
            pool.wait_ge(sumsq_done, 2 * TB)
            tab(pool.tensor_scalar(row_ss[:, :], row_ss[:, :], 1.0 / DM, EPS, ALU.mult, ALU.add))
            pool.tensor_tensor(row_r[:, :], row_ss[:, :], minus_half[:, 0:TB], ALU.pow).then_inc(row_r_done, 1)

        def rounder(act):
            def hi(w, j):
                act.wait_ge(raw_landed[j % WRAW], (w - j % WRAW) // WRAW * 32 + 32 if isinstance(w, int)
                            else 8 * (w - j % WRAW) + 32)
                if not (isinstance(w, int) and w < WSPL):
                    act.wait_ge(gemm_steps, 4 * w - 4)
                nc.scalar.activation(w_hi[:, j % WSPL], w_raw[:, j % WRAW], ACT.Copy).then_inc(w_hi_done, 1)
            return hi

        def subtracter(dve):
            def lo(w, j):
                dve.wait_ge(w_hi_done, w + 1)
                nc.vector.tensor_tensor(w_lo[:, j % WSPL], w_raw[:, j % WRAW], w_hi[:, j % WSPL].bitcast(F32),
                                        ALU.subtract).then_inc(w_lo_done, 1)
            return lo

        @block.scalar
        def _(act):
            hi = rounder(act)

            def evac(out, m, w_last, func=ACT.Copy):
                act.wait_ge(gemm_steps, 4 * w_last + m + 1)
                nc.scalar.activation(out, ps[:, m], func).then_inc(act_evac, 1)

            pin = lambda dst, src: act.dma_start(dst, src).then_inc(params_in, 16)
            by_state = lambda a: a.rearrange("o (q two) s -> (two s) (o q)", two=2)
            pin(sv[LR], by_state(t["lambda_re"]))
            pin(sv[LI], by_state(t["lambda_im"]))
            for h in range(2):
                pin(sv[DT][h * 64:(h + 1) * 64], t["log_dt"].rearrange("o (q two) -> two (o q)", two=2)[h:h + 1]
                    .to_broadcast([64, NPR]))
            for r, name in enumerate(("b_re", "b_im")):
                pin(bnat[:, r], t[name].rearrange("o (q two) s c -> (two s) (o q) c", two=2))
            for r, name in enumerate(("c_re", "c_im")):
                for h in range(2):
                    for two in range(2):
                        pin(cnat[:, r, h, two * 64:(two + 1) * 64],
                            t[name].rearrange("o (h q two) c s -> two (o h) q c s", h=2, two=2)[two, h])
            pin(masks[:, :], t["masks"])
            pin(ident[:, :], t["ident"])
            pin(eye16[:, :], t["eye16"])
            pin(gmixT[:, :], t["g_mix"].rearrange("o (k p) -> p (o k)", p=P))
            pin(gffnT[:, :], t["g_ffn"].rearrange("o (k p) -> p (o k)", p=P))
            for n, name in enumerate(("g_q", "g_k")):
                for h in range(2):
                    pin(gqk[h * 64:(h + 1) * 64, n:n + 1], t[name].rearrange("o e -> e o"))
            act.wait_ge(params_in, PARAMS)
            nc.scalar.activation(sv[DT], sv[DT], ACT.Exp).then_inc(act_tab, 1)
            act.wait_ge(dve_tab, 2)
            nc.scalar.activation(sv[MAG], sv[ZR], ACT.Exp).then_inc(act_tab, 1)
            nc.scalar.activation(sv[M8], sv[ZR], ACT.Exp, scale=float(CL)).then_inc(act_tab, 1)
            act.wait_ge(dve_tab, 10)
            nc.scalar.activation(sv[SIN], sv[RR], ACT.Sin).then_inc(act_tab, 1)
            nc.scalar.activation(sv[S2], sv[RR], ACT.Sin, scale=0.5).then_inc(act_tab, 1)
            act.wait_ge(x_loaded, 16)
            for n in range(TB):
                nc.scalar.activation(zs[:, n // 2, 2 * (n % 2):2 * (n % 2) + 2].rearrange("p a b -> p (a b)"),
                                     x_in[:, n], ACT.Square, accum_out=row_ss[:, n:n + 1]).then_inc(sumsq_done, 1)
            hi(0, 0)

            def gained(wave, g):
                for k in range(KT):
                    act.wait_ge(x_turned, KT * wave + k + 1)
                    nc.scalar.activation(hT_hi[:, k], ps[:, k], ACT.Copy, scale=g[:, k:k + 1]).then_inc(hT_hi_done, 1)

            gained(0, gmixT)
            act.wait_ge(c_turned, 1)
            nc.scalar.activation(ctr_f[:, 0:256], ps[:, 4, 0:256], ACT.Copy).then_inc(misc_act, 1)
            nc.scalar.activation(ctr_f[:, 256:512], ps[:, 5, 0:256], ACT.Copy, scale=-1.0).then_inc(misc_act, 1)

            for j in range(1, 5):
                hi(W_U + j, j)
            for m in (0, 2):
                act.wait_ge(gemm_steps, 4 * (W_V - 1) + m + 1)
                nc.scalar.activation(uT[:, m].rearrange("p (j c) -> p j c", j=CL),
                                     ps[:, m].rearrange("p (c j) -> p j c", j=CL), ACT.Copy).then_inc(act_evac, 1)

            def z_chunk(w0, c, par, free):
                for j in range(1, 5):
                    hi(w0 + 4 * c + j, j)
                act.wait_ge(z_stored, free)
                for m in (0, 2):
                    evac(zs[:, bass.ds(par, 1), m].rearrange("p b c -> p (b c)"), m, w0 + 4 * c + 3)

            for c in range(2):
                for j in range(1, 5):
                    hi(W_V + 4 * c + j, j)
                for m in (0, 2):
                    evac(zs[:, c, m], m, W_V + 4 * c + 3)
            z_chunk(W_V, 2, 0, 16)
            act.wait_ge(uc_loaded, 16 * CL)
            for f in (0, 2, 4, 6):
                act.wait_ge(w1_filled, f + 1)
                nc.scalar.activation(w1T[:, f // 4, f % 4 * 4:f % 4 * 4 + 4].rearrange("p q x -> p (q x)"),
                                     ps[:, 4 + f % 4], ACT.Copy).then_inc(misc_act, 1)
            for h in range(2):
                act.wait_ge(kall_done, h + 1)
                nc.scalar.activation(kall_f[:, h * 512:(h + 1) * 512], ps[:, 4 + h], ACT.Copy).then_inc(misc_act, 1)
            with act.Fori(0, 6) as c:
                z_chunk(W_QK, c, (c + 1) % 2, 16 * c + 32)
            for b in range(4):
                act.wait_ge(y_done, 1)
                nc.scalar.activation(ygelu[:, b // 2, b % 2 * 8:b % 2 * 8 + 8],
                                     ps[:, 4 + b].rearrange("p (q c) -> p q c", q=8), ACT.Gelu_apprx_tanh
                                     ).then_inc(misc_act, 1)

            with act.Fori(0, NPAIR // 2) as i2:
                for b in range(2):
                    i = i2 * 2 + b
                    for g in range(3):
                        act.wait_ge(qk_turned, 6 * i + g + 1)
                        nc.scalar.activation(qT[:, g], ps[:, 4 + g], ACT.Copy, scale=gqk[:, 2:3]).then_inc(misc_act, 1)
                    for u in range(9):
                        if u % 2 == 0 and u < 8:
                            hi(W_GATE + u // 2 + 1 + 4 * i, u // 2 + 1)
                        if u < 8:
                            act.wait_ge(misc_dve, MD_S + md_scores(u) + MD_PAIR * i)
                            n, h = u // 2, u % 2
                            if u >= 2:
                                act.wait_ge(prob_turned, 8 * i + u - 1)
                            k0 = 0 if n else P
                            nc.scalar.activation(prob[:, u % 2, k0:256], negs[:, u % 2, k0:256], ACT.Exp, scale=-1.0,
                                                 bias=ost[b][:, 0, n, h, HD:HD + 1],
                                                 accum_out=ost[b][:, 0, n, h, HD + 1:HD + 2])
                            nc.scalar.activation(prob[:, u % 2, 256:512], negs[:, u % 2, 256:512], ACT.Exp, scale=-1.0,
                                                 bias=ost[b][:, 1, n, h, HD:HD + 1],
                                                 accum_out=ost[b][:, 1, n, h, HD + 1:HD + 2]).then_inc(prob_done, 1)
                        if u >= 1:
                            v = u - 1
                            k0 = 0 if v // 2 else P
                            act.wait_ge(prob_turned, 8 * i + v + 1)
                            if v >= 2:
                                act.wait_ge(o_done, 8 * i + v - 1)
                            nc.scalar.activation(probT[:, v % 2, k0:512], ps[:, 6, k0:512], ACT.Copy).then_inc(misc_act, 1)
                    for m in range(4):
                        evac(gate[:, bass.ds(i * 4 + m, 1)].rearrange("p b c -> p (b c)"), m, W_GATE + 3 + 4 * i, ACT.Sigmoid)

            for b in range(2):
                act.wait_ge(o_stored[b], O_FREE)
            for m in range(4):
                nc.scalar.activation(yT_hi[:, m].rearrange("p (c i) -> p c i", i=CL),
                                     yT_raw[:, m].rearrange("p (i c) -> p c i", i=CL), ACT.Copy).then_inc(yT_hi_done, 1)
            w = W_MIX
            for c in range(2):
                hi(w + 1, w + 1)
                hi(w + 2, w + 2)
                if c:
                    act.wait_ge(glu_done, 4)
                for m in range(4):
                    evac(sgb[:, m], m, w + 1, ACT.Sigmoid)
                hi(w + 3, w + 3)
                hi(w + 4, w + 4)
                w += 4
            act.wait_ge(cmb_dve, 3)
            nc.scalar.activation(cmb[:, 1], cmb[:, 0], ACT.Exp).then_inc(cmb_act, 1)
            for k in range(4):
                act.wait_ge(a_turned, k + 1)
                nc.scalar.activation(aT_hi[:, k], ps[:, 4 + k], ACT.Copy).then_inc(aT_hi_done, 1)
            for c in range(2):
                hi(w + 1, w + 1)
                hi(w + 2, w + 2)
                for m in range(4):
                    act.wait_ge(mix_done, 4 * c + m + 1)
                    nc.scalar.activation(hT_hi[:, 4 * c + m], gate[:, 4 * c + m], ACT.Copy).then_inc(mix_hi_done, 1)
                w += 2
            for j in range(1, 9):
                hi(W_OUT + j, j)
            for n in range(TB):
                act.wait_ge(dve_evac, DE_MIX + 4 + n + 1)
                nc.scalar.activation(xn2[:, n], x1[:, n], ACT.Square, accum_out=row_ss[:, n:n + 1]).then_inc(sumsq_done, 1)
            gained(1, gffnT)
            with act.Fori(0, FB) as f:
                for j in range(1, 5):
                    hi(W_FFN + j + 4 * f, j)
                for m in range(2):
                    act.wait_ge(s_done2, 2 * f + m + 1)
                    evac(sg[:, m], m, W_FFN + 3 + 4 * f, ACT.Silu)

            def mid_hi(row, j, q):
                act.wait_ge(gemm_steps, 4 * (W_DOWN + j - 1) + 4 * q if isinstance(q, int) else 4 * (W_DOWN + j - 1) + 4 * q)
                nc.scalar.activation(yT_hi[:, j % 2], s_raw[:, bass.ds(row, 1)].rearrange("p b c -> p (b c)"),
                                     ACT.Copy).then_inc(s_hi_done, 1)

            act.wait_ge(s_done2, 2 + 2 * FB)
            mid_hi(0, 0, 0)
            with act.Fori(0, FT // 4) as q:
                for j in range(1, 5):
                    hi(W_DOWN + j + 4 * q, j)
                    mid_hi(q * 4 + j, j, 4 * q)
            hi(W_END - 1, 1)
            mid_hi(FT - 1, 1, FT - 2)
            for f in range(KT):
                act.wait_ge(down_done, f + 1)
                nc.scalar.activation(oT[:, f], ps[:, f], ACT.Copy).then_inc(down_evac, 1)

        @block.vector
        def _(dve):
            lo = subtracter(dve)
            V = nc.vector
            n_tab = [0]

            def tab(ins):
                n_tab[0] += 1
                ins.then_inc(dve_tab, 1)
                dve.wait_ge(dve_tab, n_tab[0])

            dve.wait_ge(act_tab, 1)
            tab(V.tensor_tensor(sv[ANG], sv[LI], sv[DT], ALU.mult))
            tab(V.tensor_tensor(sv[ZR], sv[LR], sv[DT], ALU.mult))
            tab(V.tensor_scalar(sv[KQ], sv[ANG], 1.0 / TWO_PI, ROUND, ALU.mult, ALU.add))
            tab(V.tensor_scalar(sv[KQ], sv[KQ], -ROUND, None, ALU.add))
            tab(V.scalar_tensor_tensor(out=sv[RR], in0=sv[KQ], scalar=-C1, in1=sv[ANG], op0=ALU.mult, op1=ALU.add))
            tab(V.scalar_tensor_tensor(out=sv[RR], in0=sv[KQ], scalar=-C2, in1=sv[RR], op0=ALU.mult, op1=ALU.add))
            tab(V.scalar_tensor_tensor(out=sv[RR], in0=sv[KQ], scalar=-C3, in1=sv[RR], op0=ALU.mult, op1=ALU.add))
            tab(V.tensor_scalar(sv[RR], sv[RR], PI_BELOW, -PI_BELOW, ALU.min, ALU.max))
            tab(V.tensor_tensor(sv[DEN], sv[LR], sv[LR], ALU.mult))
            tab(V.tensor_tensor(sv[SQ], sv[LI], sv[LI], ALU.mult))
            tab(V.tensor_tensor(sv[DEN], sv[DEN], sv[SQ], ALU.add))
            tab(V.reciprocal(sv[RD], sv[DEN]))
            tab(V.tensor_tensor(gqk[:, 2:3], gqk[:, 0:1], gqk[:, 1:2], ALU.mult))
            tab(V.tensor_scalar(gqk[:, 2:3], gqk[:, 2:3], HD ** -0.5, None, ALU.mult))
            dve.wait_ge(dsk_in, 128)
            V.tensor_tensor(dadd, eye16[:, :].unsqueeze(1).to_broadcast([P, 8, CH]),
                            dsk.unsqueeze(2).to_broadcast([P, 8, CH]), ALU.mult).then_inc(dve_tab, 1)

            def turn_lo(wave, g):
                for k in range(KT):
                    dve.wait_ge(hT_hi_done, KT * wave + k + 1)
                    V.scalar_tensor_tensor(out=hT_lo[:, k], in0=ps[:, k], scalar=g[:, k:k + 1],
                                           in1=hT_hi[:, k].bitcast(F32), op0=ALU.mult, op1=ALU.subtract
                                           ).then_inc(hT_lo_done, 1)

            def evac(out, m, w_last):
                dve.wait_ge(gemm_steps, 4 * w_last + m + 1)
                V.tensor_copy(out, ps[:, m]).then_inc(dve_evac, 1)

            dve.wait_ge(row_r_done, 1)
            for n in range(TB):
                V.tensor_scalar(x_in[:, n], x_in[:, n], row_r[:, n:n + 1], None, ALU.mult).then_inc(xn_done, 1)
            lo(0, 0)
            turn_lo(0, gmixT)
            for j in range(1, 5):
                lo(W_U + j, j)
            for m in (1, 3):
                dve.wait_ge(gemm_steps, 4 * (W_V - 1) + m + 1)
                V.tensor_copy(uT[:, m].rearrange("p (j c) -> p j c", j=CL),
                              ps[:, m].rearrange("p (c j) -> p j c", j=CL)).then_inc(dve_evac, 1)
            for c in range(2):
                for j in range(1, 5):
                    lo(W_V + 4 * c + j, j)
                for m in (1, 3):
                    evac(zs[:, c, m], m, W_V + 4 * c + 3)
            for j in range(1, 5):
                lo(W_V + 8 + j, j)
            dve.wait_ge(z_stored, 16)
            for m in (1, 3):
                evac(zs[:, 0, m], m, W_V + 11)
            dve.wait_ge(uc_loaded, 16 * CL)
            for f in (1, 3, 5, 7):
                dve.wait_ge(w1_filled, f + 1)
                V.tensor_copy(w1T[:, f // 4, f % 4 * 4:f % 4 * 4 + 4].rearrange("p q x -> p (q x)"),
                              ps[:, 4 + f % 4]).then_inc(misc_dve, 1)
            dve.wait_ge(dve_tab, n_tab[0] + 1)
            for h in range(2):
                dve.wait_ge(misc_act, MA_W1 + h + 1)
                kd = kall[:, h, :, 0:CH]
                V.tensor_tensor(kd, kd, dadd[:, 4 * h:4 * h + 4], ALU.add).then_inc(kall_out, 1)

            def z_chunk(c, w0, free, first):
                for j in range(1, 5):
                    lo(w0 + 4 * c + j, j)
                    if j == 2 and not first:
                        z_sums(c - 1)
                dve.wait_ge(z_stored, free)
                for m in (1, 3):
                    evac(zs[:, bass.ds((c + 1) % 2, 1), m].rearrange("p b c -> p (b c)"), m, w0 + 4 * c + 3)

            def z_sums(c):
                dve.wait_ge(z_sq, c + 1)
                V.tensor_reduce(z_ss, zsq[:, 0:2048].rearrange("p (g e) -> p g e", e=HD), AX_X, ALU.add
                                ).then_inc(z_sum, 1)

            z_chunk(0, W_QK, 32, True)
            with dve.Fori(1, 3) as c:
                z_chunk(c, W_QK, 16 * c + 32, False)

            n_scan = [0]

            def scan(ins, sync=True):
                n_scan[0] += 1
                ins.then_inc(scan_step, 1)
                if sync:
                    dve.wait_ge(scan_step, n_scan[0])

            s_re = ps[:, 4:6, :].rearrange("p b x -> p (b x)")
            s_im = ps[:, 6:8, :].rearrange("p b x -> p (b x)")
            r_re, r_im = rot_f[:, 0:1024], rot_f[:, 1024:2048]
            tmp = kall_f
            zr, zi, yr, yi = turned
            dve.wait_ge(s_done, 1)
            dve.wait_ge(pool_tab, TAB["all"])
            dve.wait_ge(k_stored, 128)
            scan(V.tensor_tensor(zr, s_re, r_re, ALU.mult), False)
            scan(V.tensor_tensor(tmp, s_im, r_im, ALU.mult))
            scan(V.tensor_tensor(zr, zr, tmp, ALU.add))
            scan(V.tensor_tensor(zi, s_im, r_re, ALU.mult), False)
            V.tensor_tensor(tmp, s_re, r_im, ALU.mult).then_inc(misc_dve, 1)
            dve.wait_ge(misc_dve, MD_S)
            scan(V.tensor_tensor(zi, zi, tmp, ALU.subtract))
            scan(V.tensor_tensor_scan(yr, m8row_f, zr, 0.0, ALU.mult, ALU.add), False)
            scan(V.tensor_tensor_scan(yi, m8row_f, zi, 0.0, ALU.mult, ALU.add))
            grid = lambda a: a.rearrange("p (q c) -> p q c", q=NPR)
            cut_c = lambda a: grid(a)[:, :, 0:NC - 1]
            x_re, x_im = xst[:, 0, :, 1:NC], xst[:, 1, :, 1:NC]
            scan(V.tensor_tensor(x_re, cut_c(yr), cut_c(r_re), ALU.mult), False)
            scan(V.tensor_tensor(cut_c(tmp), cut_c(yi), cut_c(r_im), ALU.mult))
            scan(V.tensor_tensor(x_re, x_re, cut_c(tmp), ALU.subtract))
            scan(V.tensor_tensor(x_im, cut_c(yi), cut_c(r_re), ALU.mult), False)
            scan(V.tensor_tensor(cut_c(tmp), cut_c(yr), cut_c(r_im), ALU.mult))
            V.tensor_tensor(x_im, x_im, cut_c(tmp), ALU.add).then_inc(xst_done, 1)

            with dve.Fori(3, 6) as c:
                z_chunk(c, W_QK, 16 * c + 32, False)
            z_sums(5)

            def add_o(u, b):
                n, h = u // 2, u % 2
                return V.tensor_copy(ost[b][:, :, n, h, 0:HD],
                                     ps[:, 7, (u % 4) * P:(u % 4 + 1) * P].rearrange("p (s e) -> p s e", s=2)
                                     ).then_inc(misc_dve, 1)

            with dve.Fori(0, NPAIR // 2) as i2:
                for b in range(2):
                    i = i2 * 2 + b
                    for g in range(3):
                        dve.wait_ge(qk_turned, 6 * i + g + 4)
                        V.tensor_copy(kT[:, g], ps[:, 4 + (3 + g) % 4]).then_inc(misc_dve, 1)
                    for u in range(10):
                        if u % 2 == 0 and u < 8:
                            lo(W_GATE + u // 2 + 1 + 4 * i, u // 2 + 1)
                        if u == 0:
                            dve.wait_ge(o_stored[b], 80 * i2 + O_FREE)
                        if u < 8:
                            n, h = u // 2, u % 2
                            wait_apart(dve, (scores_done, 8 * i + u + 1),
                                       *([(prob_done, 8 * i + u - 1)] if u >= 2 else []))
                            k0 = 0 if n else P
                            V.tensor_tensor_reduce(negs[:, u % 2, k0:256], ps[:, 4 + u % 2, k0:256], masks[:, k0:256],
                                                   -1.0, 3.0e38, ALU.add, ALU.min, ost[b][:, 0, n, h, HD:HD + 1])
                            V.tensor_tensor_reduce(negs[:, u % 2, 256:512], ps[:, 4 + u % 2, 256:512], masks[:, 256:512],
                                                   -1.0, 3.0e38, ALU.add, ALU.min, ost[b][:, 1, n, h, HD:HD + 1]
                                                   ).then_inc(misc_dve, 1)
                        if u >= 2:
                            dve.wait_ge(o_done, 8 * i + u - 1)
                            add_o(u - 2, b)

            for m in range(4):
                dve.wait_ge(yT_hi_done, m + 1)
                V.tensor_tensor(yT_lo[:, m].rearrange("p (c i) -> p c i", i=CL),
                                yT_raw[:, m].rearrange("p (i c) -> p c i", i=CL),
                                yT_hi[:, m].bitcast(F32).rearrange("p (c i) -> p c i", i=CL), ALU.subtract
                                ).then_inc(yT_lo_done, 1)
            n_cmb = [0]

            def step(ins, sync=True):
                n_cmb[0] += 1
                ins.then_inc(cmb_dve, 1)
                if sync:
                    dve.wait_ge(cmb_dve, n_cmb[0])

            stat = lambda s, e: oall[:, s, :, :, HD + e]
            wide = lambda a: a.unsqueeze(3).to_broadcast([P, TB, 8, HD])

            def combine():
                dve.wait_ge(oall_in, 128)
                step(V.tensor_tensor(cmb[:, 2, 0], stat(0, 0), stat(1, 0), ALU.min))
                for s in range(2):
                    step(V.tensor_tensor(cmb[:, 0, s], cmb[:, 2, 0], stat(s, 0), ALU.subtract), s == 1)
                dve.wait_ge(cmb_act, 1)
                for s in range(2):
                    step(V.tensor_tensor(cmb[:, 3, s], cmb[:, 1, s], stat(s, 1), ALU.mult), s == 1)
                step(V.tensor_tensor(cmb[:, 2, 0], cmb[:, 3, 0], cmb[:, 3, 1], ALU.add))
                step(V.reciprocal(cmb[:, 2, 1], cmb[:, 2, 0]))
                for s in range(2):
                    step(V.tensor_tensor(cmb[:, 4, s], cmb[:, 1, s], cmb[:, 2, 1], ALU.mult), s == 1)
                step(V.tensor_tensor(a_tok, oall[:, 0, :, :, 0:HD], wide(cmb[:, 4, 0]), ALU.mult), False)
                step(V.tensor_tensor(a_tmp, oall[:, 1, :, :, 0:HD], wide(cmb[:, 4, 1]), ALU.mult))
                V.tensor_tensor(a_tok, a_tok, a_tmp, ALU.add).then_inc(a_ready, 1)

            w = W_MIX
            for c in range(2):
                lo(w + 1, w + 1)
                lo(w + 2, w + 2)
                lo(w + 3, w + 3)
                lo(w + 4, w + 4)
                for m in range(4):
                    dve.wait_ge(gemm_steps, 4 * (w + 3) + m + 1)
                    dve.wait_ge(act_evac, AE_G + 4 * c + m + 1)
                    V.tensor_tensor(sgb[:, m], sgb[:, m], ps[:, m], ALU.mult).then_inc(dve_evac, 1)
                w += 4
                if c == 1:
                    combine()
            for k in range(4):
                dve.wait_ge(aT_hi_done, k + 1)
                V.tensor_tensor(aT_lo[:, k], ps[:, 4 + k], aT_hi[:, k].bitcast(F32), ALU.subtract).then_inc(aT_lo_done, 1)
            for c in range(2):
                lo(w + 1, w + 1)
                lo(w + 2, w + 2)
                for m in range(4):
                    dve.wait_ge(gemm_steps, 4 * (w + 1) + m + 1)
                    ga = gate[:, 4 * c + m]
                    V.tensor_tensor(ga, ga, ps[:, m], ALU.mult).then_inc(dve_evac, 1)
                    dve.wait_ge(dve_evac, DE_GLU + 4 * c + m + 1)
                    dve.wait_ge(glu_done, 4 * c + m + 1)
                    V.tensor_tensor(ga, ga, gate[:, 8 + 4 * c + m], ALU.add).then_inc(mix_done, 1)
                for m in range(4):
                    dve.wait_ge(mix_hi_done, 4 * c + m + 1)
                    V.tensor_tensor(hT_lo[:, 4 * c + m], gate[:, 4 * c + m], hT_hi[:, 4 * c + m].bitcast(F32),
                                    ALU.subtract).then_inc(mix_lo_done, 1)
                w += 2
            dve.wait_ge(x1_in, 16)
            for c in range(2):
                for j in range(1, 5):
                    lo(W_OUT + 4 * c + j, j)
                for n in range(TB):
                    dve.wait_ge(gemm_steps, 4 * (W_OUT + 4 * c + 3) + n + 1)
                    xh = x1[:, n, c * 512:(c + 1) * 512]
                    V.tensor_tensor(xh, xh, ps[:, n], ALU.add).then_inc(dve_evac, 1)
            dve.wait_ge(row_r_done, 2)
            for n in range(TB):
                V.tensor_scalar(xn2[:, n], x1[:, n], row_r[:, n:n + 1], None, ALU.mult).then_inc(xn_done, 1)
            turn_lo(1, gffnT)
            V.engine_nop().then_inc(s_done2, 1)
            V.engine_nop().then_inc(s_done2, 1)
            with dve.Fori(0, FB) as f:
                for j in range(1, 5):
                    lo(W_FFN + j + 4 * f, j)
                for m in range(2):
                    dve.wait_ge(act_evac, AE_GLU + m + 1 + 2 * f)
                    dve.wait_ge(gemm_steps, 4 * (W_FFN + 3) + 2 + m + 1 + 16 * f)
                    V.tensor_tensor(s_raw[:, bass.ds(f * 2 + m, 1)].rearrange("p b c -> p (b c)"), sg[:, m],
                                    ps[:, 2 + m], ALU.mult).then_inc(s_done2, 1)

            def mid_lo(row, j):
                dve.wait_ge(s_hi_done, row + 1)
                V.tensor_tensor(yT_lo[:, j % 2], s_raw[:, bass.ds(row, 1)].rearrange("p b c -> p (b c)"),
                                yT_hi[:, j % 2].bitcast(F32), ALU.subtract).then_inc(s_lo_done, 1)

            dve.wait_ge(s_done2, 2 + 2 * FB)
            mid_lo(0, 0)
            with dve.Fori(0, FT // 4) as q:
                for j in range(1, 5):
                    lo(W_DOWN + j + 4 * q, j)
                    mid_lo(q * 4 + j, j)
            lo(W_END - 1, 1)
            mid_lo(FT - 1, 1)
            for f in range(KT):
                dve.wait_ge(out_turned, f + 1)
                cols_f = slice(f * P, (f + 1) * P)
                V.tensor_tensor(y_out[:, :, cols_f], x1[:, :, cols_f], ps[:, f].rearrange("p (n c) -> p n c", n=TB),
                                ALU.add).then_inc(out_done, 1)

        @block.tensor
        def _(pe):
            T = nc.tensor

            def products(w, j, first, last, operands, bank_free):
                for m in range(4):
                    if m == 0:
                        pe.wait_ge(w_lo_done, w + 1)
                    if first:
                        bank_free(m)
                    for h in range(2):
                        for k, (a, b) in enumerate(((0, 0), (1, 0), (0, 1))):
                            lhsT, rhs = operands(m, h, (w_hi, w_lo)[b][:, j % WSPL, h * 512:(h + 1) * 512], a)
                            ins = T.matmul(ps[:, m], lhsT, rhs, start=first and h == 0 and k == 0,
                                           stop=last and h == 1 and k == 2)
                    ins.then_inc(gemm_steps, 1)
                    yield

            def by_token(acts, j):
                return lambda m, h, w, a: (acts[a][:, 2 * j + h, m * P:(m + 1) * P], w)

            def by_feature(acts, j):
                return lambda m, h, w, a: (w[:, m * P:(m + 1) * P], acts[a][:, 2 * j + h, :])

            def columns(w0, n, how, acts, bank_free):
                for j in range(n):
                    jj = j if not isinstance(w0, int) else w0 + j
                    yield from products(w0 + j, jj, j == 0, j == n - 1, how(acts, j), bank_free)

            def run(gen):
                for _ in gen:
                    pass

            h_acts, y_acts, a_acts = (hT_hi, hT_lo), (yT_hi, yT_lo), (aT_hi, aT_lo)

            def rows_turned(wave, src):
                for n in range(TB):
                    pe.wait_ge(xn_done, TB * wave + n + 1)
                    for k in range(KT):
                        ins = T.transpose(ps[:, k, n * P:(n + 1) * P], src[:, n, k * P:(k + 1) * P], ident[:, :])
                        if n == TB - 1:
                            ins.then_inc(x_turned, 1)

            pe.wait_ge(params_in, PARAMS)
            rows_turned(0, x_in)
            pe.wait_ge(hT_lo_done, KT)
            for r in range(2):
                for h in range(2):
                    ins = T.transpose(ps[:, 4 + r, h * P:(h + 1) * P], cnat[:, r, h], ident[:, :])
            ins.then_inc(c_turned, 1)
            run(columns(W_U, 4, by_feature, h_acts, lambda m: None))

            def alternating(a0, d0):
                def free(m):
                    pe.wait_ge(act_evac if m % 2 == 0 else dve_evac, (a0 if m % 2 == 0 else d0) + m // 2 + 1)
                return free

            with pe.Fori(0, 3) as c:
                run(columns(W_V + 4 * c, 4, by_token, h_acts, alternating(2 * c, 2 * c)))

            pe.wait_ge(pool_tab, TAB["ca"])
            pe.wait_ge(misc_act, MA_C)
            for f in range(8):
                if f >= 4:
                    pe.wait_ge(misc_act if f % 2 == 0 else misc_dve, (MA_C if f % 2 == 0 else 0) + (f - 4) // 2 + 1)
                for x in range(4):
                    ins = T.transpose(ps[:, 4 + f % 4, x * P:(x + 1) * P],
                                      aB[:, f // 4, f % 4 * 4 + x].rearrange("p k c -> p (k c)"), ident[:, :])
                ins.then_inc(w1_filled, 1)
            for h in range(2):
                pe.wait_ge(misc_act if h == 0 else misc_dve, (MA_C if h == 0 else 0) + 3)
                rows = slice(64 * h, 64 * h + 64)
                for q in range(NPR):
                    for r in range(2):
                        ins = T.matmul(ps[32 * (q % 4):32 * (q % 4) + 32, 4 + h, q // 4 * P:(q // 4 + 1) * P],
                                       bb[rows, r, q:q + 2].rearrange("p q c -> p (q c)"),
                                       ca[rows, r, q, 0:CL].rearrange("p k c -> p (k c)"),
                                       start=r == 0, stop=r == 1)
                ins.then_inc(kall_done, 1)

            with pe.Fori(0, 3) as c:
                run(columns(W_QK + 4 * c, 4, by_token, h_acts, alternating(AE_U + 4 + 2 * c, DE_U + 4 + 2 * c)))
            pe.wait_ge(uc_loaded, 16 * CL)
            pe.wait_ge(misc_act, MA_K)
            pe.wait_ge(misc_dve, MD_W1)
            for r in range(2):
                for q in range(NPR):
                    for h in range(2):
                        ins = T.matmul(ps[64 * h:64 * h + 64, 4 + 2 * r + q // 8, q % 8 * NC:(q % 8 + 1) * NC],
                                       w1T[:, r, q, 64 * h:64 * h + 64], uc[:, 2 * q + h], start=True, stop=True)
            ins.then_inc(s_done, 1)
            with pe.Fori(3, 6) as c:
                run(columns(W_QK + 4 * c, 4, by_token, h_acts, alternating(AE_U + 4 + 2 * c, DE_U + 4 + 2 * c)))
            pe.wait_ge(xst_done, 1)
            pe.wait_ge(toep_in, 16 * CL)
            for h in range(2):
                rows = slice(64 * h, 64 * h + 64)
                for q in range(NPR):
                    out = ps[:, 4 + 2 * h + q // 8, q % 8 * NC:(q % 8 + 1) * NC]
                    T.matmul(out, toep[:, 2 * q + h], uc[:, 2 * q + h], start=True, stop=False)
                    for r in range(2):
                        ins = T.matmul(out, ca[rows, r, q, 1:CL + 1].rearrange("p k c -> p (k c)"),
                                       xst[rows, r, q, 0:NC], start=False, stop=r == 1)
            ins.then_inc(y_done, 1)

            def scores(i, u):
                n, h = u // 2, u % 2
                rows = slice(64 * h, 64 * h + 64)
                if u >= 2:
                    pe.wait_ge(misc_dve, MD_S + md_scores(u - 2) + MD_PAIR * i)
                k0 = 0 if n else P
                q = slice(n * P, (n + 1) * P)
                bank = 4 + u % 2
                T.matmul(ps[:, bank, k0:256], qT[rows, 0, q], kT[rows, 0, n * P - P + k0:n * P + P],
                         start=True, stop=True)
                for g in (1, 2):
                    ins = T.matmul(ps[:, bank, (g + 1) * P:(g + 2) * P], qT[rows, g, q], kT[rows, g, q],
                                   start=True, stop=True)
                ins.then_inc(scores_done, 1)

            def turn_prob(i, u):
                pe.wait_ge(prob_done, 8 * i + u + 1)
                if u:
                    pe.wait_ge(misc_act, MA_Y + ma_probT(u - 1) + MA_PAIR * i)
                for x in range(0 if u // 2 else 1, 4):
                    ins = T.transpose(ps[:, 6, x * P:(x + 1) * P], prob[:, u % 2, x * P:(x + 1) * P], ident[:, :])
                ins.then_inc(prob_turned, 1)

            def values(i, u, b):
                n, h = u // 2, u % 2
                pe.wait_ge(misc_act, MA_Y + ma_probT(u) + MA_PAIR * i)
                if u == 0:
                    pe.wait_ge(zt_v_in, 16 * 9 * i + 16 * 9)
                if u:
                    pe.wait_ge(misc_dve, MD_S + md_out(u - 1) + MD_PAIR * i)
                e = slice(h * HD, (h + 1) * HD)
                terms = ([(0, 0, n - 1)] if n else []) + [(0, 1, n), (1, 2, n), (1, 3, n)]
                for x, (s, blk, key) in enumerate(terms):
                    g = (0, 0, 1, 2)[blk]
                    ins = T.matmul(ps[:, 7, (u % 4) * P + s * HD:(u % 4) * P + (s + 1) * HD],
                                   probT[:, u % 2, blk * P:(blk + 1) * P], vt[b][:, g, key, e],
                                   start=blk in ((0 if n else 1), 2), stop=blk in (1, 3))
                ins.then_inc(o_done, 1)

            with pe.Fori(0, NPAIR // 2) as i2:
                for b in range(2):
                    i = i2 * 2 + b
                    pe.wait_ge(zt_qk_in, 16 * 18 * i + 16 * 18)
                    pe.wait_ge(misc_act, MA_Y + MA_PAIR * i)
                    pe.wait_ge(misc_dve, MD_S + MD_PAIR * i)
                    for s in range(6):
                        if s >= 4:
                            pe.wait_ge(misc_act, MA_Y + s - 3 + MA_PAIR * i)
                        for n in range(TB):
                            ins = T.transpose(ps[:, 4 + s % 4, n * P:(n + 1) * P], zt[:, s, n], ident[:, :])
                        ins.then_inc(qk_turned, 1)
                    pe.wait_ge(misc_act, MA_Y + 3 + MA_PAIR * i)
                    pe.wait_ge(misc_dve, MD_S + 3 + MD_PAIR * i)

                    def gate_bank_free(m):
                        if m % 2:
                            pe.wait_ge(dve_evac, DE_Z - 1 + m // 2)
                            pe.wait_ge(act_evac, AE_Z + 4 * i)
                        else:
                            pe.wait_ge(act_evac, AE_Z + 4 * i)
                    gates = columns(W_GATE + 4 * i, 4, by_feature, h_acts, gate_bank_free)
                    for u in range(10):
                        if u < 8:
                            scores(i, u)
                            next(gates)
                            next(gates)
                        if 1 <= u < 9:
                            turn_prob(i, u - 1)
                        if u >= 2:
                            values(i, u - 2, b)
                    run(gates)

            def by_act(a0):
                return lambda m: pe.wait_ge(act_evac, a0 + m + 1)

            def by_dve(d0):
                return lambda m: pe.wait_ge(dve_evac, d0 + m + 1)

            pe.wait_ge(yT_lo_done, 4)
            w = W_MIX
            for c in range(2):
                run(columns(w, 2, by_feature, y_acts, by_act(AE_G - 4) if c == 0 else by_dve(DE_Z)))
                run(columns(w + 2, 2, by_feature, y_acts, by_act(AE_G + 4 * c)))
                w += 4
            pe.wait_ge(a_ready, 1)
            pe.wait_ge(misc_act, MA_ATT)
            pe.wait_ge(misc_dve, MD_ATT)
            for k in range(4):
                for n in range(TB):
                    ins = T.transpose(ps[:, 4 + k, n * P:(n + 1) * P],
                                      a_tok[:, n, 2 * k:2 * k + 2].rearrange("p g e -> p (g e)"), ident[:, :])
                ins.then_inc(a_turned, 1)
            pe.wait_ge(aT_lo_done, 4)
            for c in range(2):
                run(columns(w, 2, by_feature, a_acts, by_dve(DE_Z + 4 + 4 * c)))
                w += 2
            pe.wait_ge(mix_lo_done, 8)
            for c in range(2):
                run(columns(W_OUT + 4 * c, 4, by_token, h_acts, by_dve(DE_GLU + 4 + 4 * c)))
            rows_turned(1, xn2)
            pe.wait_ge(hT_lo_done, 2 * KT)

            def ffn_free(f):
                def free(m):
                    if m < 2:
                        pe.wait_ge(act_evac, AE_GLU - 2 + m + 1 + 2 * f)
                    else:
                        pe.wait_ge(dve_evac, DE_OUT - 2 + m - 1 + 2 * f)
                return free

            def by_half(acts, j):
                return lambda m, h, w, a: (w[m // 2][:, h * 256 + m % 2 * P:h * 256 + (m % 2 + 1) * P],
                                           acts[a][:, 2 * j + h, :])

            with pe.Fori(0, FB) as f:
                for j in range(4):
                    w = W_FFN + j + 4 * f
                    pe.wait_ge(w_lo_done, w + 1)
                    for m in range(4):
                        if j == 0:
                            if m < 2:
                                pe.wait_ge(act_evac, AE_GLU - 1 + m + 2 * f)
                            else:
                                pe.wait_ge(s_done2, 2 * f + m - 1)
                        for h in range(2):
                            for k, (a, b) in enumerate(((0, 0), (1, 0), (0, 1))):
                                at_w = m // 2 * 512 + h * 256 + m % 2 * P
                                ins = T.matmul(ps[:, m], (w_hi, w_lo)[b][:, j % WSPL, at_w:at_w + P],
                                               h_acts[a][:, 2 * j + h, :], start=j == 0 and h == 0 and k == 0,
                                               stop=j == 3 and h == 1 and k == 2)
                        ins.then_inc(gemm_steps, 1)

            def down(w, j, row, first, last):
                pe.wait_ge(w_lo_done, w + 1)
                pe.wait_ge(s_lo_done, row + 1)
                for m in range(KT):
                    for k, (a, b) in enumerate(((0, 0), (1, 0), (0, 1))):
                        ins = T.matmul(ps[:, m], (w_hi, w_lo)[b][:, j % WSPL, m * P:(m + 1) * P],
                                       y_acts[a][:, j % 2, :], start=first and k == 0, stop=last and k == 2,
                                       skip_group_check=not (first or last))
                    if last:
                        ins.then_inc(down_done, 1)
                    elif m % 2:
                        ins.then_inc(gemm_steps, 1)

            pe.wait_ge(act_evac, AE_F)
            down(W_DOWN, 0, 0, True, False)
            with pe.Fori(0, (FT - 2) // 4) as q:
                for j in range(1, 5):
                    down(W_DOWN + j + 4 * q, j, q * 4 + j, False, False)
            down(W_END - 1, 1, FT - 1, False, True)
            for f in range(KT):
                pe.wait_ge(down_evac, f + 1)
                for n in range(TB):
                    ins = T.transpose(ps[:, f, n * P:(n + 1) * P], oT[:, f, n * P:(n + 1) * P], ident[:, :])
                ins.then_inc(out_turned, 1)


def constants():
    q = np.arange(P)[:, None]
    k = np.arange(P)[None, :]
    tq, tk = 4 * (q % 32) + q // 32, 4 * (k % 32) + k // 32
    allowed = [k >= q, k <= q, tk <= tq, (q // 32 == k // 32) & (k <= q)]
    masks = np.concatenate([np.where(a, 0.0, NEG) for a in allowed], axis=1).astype(np.float32)
    return {"masks": masks, "ident": np.eye(P, dtype=np.float32),
            "eye16": (q % 32 == np.arange(CH)[None, :]).astype(np.float32)}


def kernel(**inputs):
    import concourse.bacc as _bacc
    from concourse.bass_utils import run_bass_kernel_spmd as _run

    nc = _bacc.Bacc("TRN2", target_bir_lowering=False, num_devices=1)
    arrays, dram = {}, {}
    for name, a in {**inputs, **constants()}.items():
        a = np.ascontiguousarray(a)
        if name.startswith("w_"):
            a = a[0]
        arrays["in_" + name] = a
        dram[name] = nc.dram_tensor("in_" + name, a.shape, mybir.dt.from_np(a.dtype), kind="ExternalInput").ap()
    dram["out"] = nc.dram_tensor("out_0", (1, SEQ, DM), F32, kind="ExternalOutput").ap()
    build(nc, dram)
    r = _run(nc, [arrays], core_ids=[0])
    return r.results[0]["out_0"]
```

```python
from contextlib import ExitStack

import numpy as np

import concourse.bass as bass
from concourse import mybir

F32 = mybir.dt.float32
F32R = mybir.dt.float32r
ALU = mybir.AluOpType
ACT = mybir.ActivationFunctionType
AX_X = mybir.AxisListType.X

P = 128
SEQ = 512
DM = 1024
TB = SEQ // P
KT = DM // P
HD = 64
NPAIR = 4
AW = 512
FF = 2816
FT = FF // P
FB = FF // 256
EPS = 1e-6
NG = 32
NPR = NG // 2
CH = 16
CL = 8
NC = SEQ // CL
WRAW = 4
WSPL = 2
OW = HD + 2

W_U = 0
W_V = W_U + 4
W_QK = W_V + 12
W_GATE = W_QK + 24
W_MIX = W_GATE + 16
W_OUT = W_MIX + 12
W_FFN = W_OUT + 8
W_DOWN = W_FFN + 4 * FB
W_END = W_DOWN + FT

TWO_PI = 6.283185307179586
C1 = 6.28125
C2 = 0.0019350051879882812
C3 = TWO_PI - C1 - C2
ROUND = 12582912.0
PI_BELOW = 3.1415925
NEG = -1.0e30


N_PARAMS = 21
PARAMS = 16 * N_PARAMS


def build(nc, t):
    with ExitStack() as ctx:
        sems = {}

        def sem(name):
            if name not in sems:
                sems[name] = ctx.enter_context(nc.semaphore(name))
            return sems[name]

        def sb(stack, name, shape, dt=F32):
            return stack.enter_context(nc.sbuf_tensor(name, shape, dt))

        hT_hi = sb(ctx, "hT_hi", [P, KT, SEQ], F32R)
        hT_lo = sb(ctx, "hT_lo", [P, KT, SEQ], F32R)
        w_raw = sb(ctx, "w_raw", [P, WRAW, 1024])
        w_hi = sb(ctx, "w_hi", [P, WSPL, 1024], F32R)
        w_lo = sb(ctx, "w_lo", [P, WSPL, 1024], F32R)
        masks = sb(ctx, "masks", [P, 4 * P])
        ident = sb(ctx, "ident", [P, P])
        eye16 = sb(ctx, "eye16", [P, CH])
        gmixT = sb(ctx, "gmixT", [P, KT])
        gffnT = sb(ctx, "gffnT", [P, KT])
        gqk = sb(ctx, "gqk", [P, 3])
        row_ss = sb(ctx, "row_ss", [P, TB])
        row_ss2 = sb(ctx, "row_ss2", [P, TB])
        row_r = sb(ctx, "row_r", [P, TB])
        minus_half = sb(ctx, "minus_half", [P, 32])


        with nc.sbuf_tensor("early", [P, 34816], F32) as early:
            pass
        at = [0]

        def cut(arena, n, at=at):
            at[0] += n
            return arena[:, at[0] - n:at[0]]

        x_in_f = cut(early, TB * DM)
        zs = cut(early, 2 * TB * AW).rearrange("p (b m c) -> p b m c", b=2, m=TB)
        spare = cut(early, 2 * 2 * P)
        cnat = spare.rearrange("p (r h x) -> p r h x", r=2, h=2)
        ctr_f = cut(early, 2 * NPR * CH)
        bnat = cut(early, 2 * NPR * CH).rearrange("p (r q c) -> p r q c", r=2, q=NPR)
        bb_f = cut(early, 2 * (NPR + 1) * CH)
        m8row_f = cut(early, NPR * NC)
        aB_f = cut(early, 2 * NPR * CL * CH)
        ca = cut(early, 2 * NPR * (CL + 1) * CH).rearrange("p (r q k c) -> p r q k c", r=2, q=NPR, k=CL + 1)
        toep_f = cut(early, NG * CL * CH)
        rot_f = cut(early, 2 * NPR * NC)
        uc_f = cut(early, NG * NC)
        kall_f = cut(early, 1024)
        dsk = cut(early, 4)
        dadd = cut(early, 4 * CH).rearrange("p (g c) -> p g c", g=4)
        states = cut(early, 24 * NPR).rearrange("p (n q) -> p n q", n=24)
        apw = cut(early, 2 * (CL + 1) * NPR).rearrange("p (r k q) -> p r k q", r=2, k=CL + 1)
        apn = cut(early, (CL + 1) * NPR).rearrange("p (k q) -> p k q", k=CL + 1)
        z_ss = cut(early, 32)
        z_r = cut(early, 32)
        z_t = cut(early, 32)
        zsq = cut(early, 2304)
        x_in = x_in_f.rearrange("p (n c) -> p n c", n=TB)
        uT = x_in_f[:, 0:4 * SEQ].rearrange("p (m x) -> p m x", m=4)
        w1T = x_in_f.rearrange("p (r q x) -> p r q x", r=2, q=NPR)
        aB = aB_f.rearrange("p (r q k c) -> p r q k c", r=2, q=NPR, k=CL)
        toep = toep_f.rearrange("p (g x) -> p g x", g=NG)
        rot = rot_f.rearrange("p (r q c) -> p r q c", r=2, q=NPR)
        uc = uc_f.rearrange("p (g c) -> p g c", g=NG)
        m8row = m8row_f.rearrange("p (q c) -> p q c", q=NPR)
        ctr = ctr_f.rearrange("p (r q c) -> p r q c", r=2, q=NPR)
        bb = bb_f.rearrange("p (r q c) -> p r q c", r=2, q=NPR + 1)
        kall = kall_f[:, 0:512].rearrange("p (q x) -> p q x", q=4)
        bb2 = zsq[:, 0:2 * NPR * 2 * CH].rearrange("p (r q h c) -> p r q h c", r=2, q=NPR, h=2)
        xst = x_in_f.rearrange("p (r q h c) -> p r q h c", r=2, q=NPR, h=2)
        turned = [aB_f[:, n * 1024:(n + 1) * 1024] for n in range(4)]
        ygelu = rot_f
        LR, LI, DT, ZR, ANG, KQ, RR, DEN, SQ, RD, MAG, M8, SIN, S2, COS, NR, T1, T2, CR, CI, ER, EI, FR, FI = range(24)
        sv = [states[:, n, :] for n in range(24)]

        late_stack = ExitStack()
        yT_hi = sb(late_stack, "yT_hi", [P, 4, SEQ], F32R)
        yT_lo = sb(late_stack, "yT_lo", [P, 4, SEQ], F32R)
        aT_hi = sb(late_stack, "aT_hi", [P, 4, SEQ], F32R)
        aT_lo = sb(late_stack, "aT_lo", [P, 4, SEQ], F32R)
        late = sb(late_stack, "late", [P, 26624])
        late_stack.close()
        off = lambda a, n: late[:, a:a + n]
        zt = off(0, 3072).rearrange("p (s n c) -> p s n c", s=6, n=TB)
        V_AT, V_STEP = 3072, 12544
        vt = [off(V_AT + b * V_STEP, 1536).rearrange("p (g n c) -> p g n c", g=3, n=TB) for b in range(2)]
        qT = off(4608, 1536).rearrange("p (g t) -> p g t", g=3)
        kT = off(6144, 1536).rearrange("p (g t) -> p g t", g=3)
        negs = off(7680, 1024).rearrange("p (b k) -> p b k", b=2)
        prob = off(8704, 1024).rearrange("p (b k) -> p b k", b=2)
        probT = off(9728, 1024).rearrange("p (b k) -> p b k", b=2)
        ost = [off(a, 1056).rearrange("p (s n h e) -> p s n h e", s=2, n=TB, h=2) for a in (10752, 25344)]
        yT_raw = off(11808, 2048).rearrange("p (m x) -> p m x", m=4)
        gate = off(17152, 8192).rearrange("p (m t) -> p m t", m=16)
        oall = off(0, 4224).rearrange("p (s n g e) -> p s n g e", s=2, n=TB, g=8)
        oall_d = off(0, 4224).rearrange("p (s n i x) -> p s n i x", s=2, n=TB, i=NPAIR)
        a_tok = off(4608, 2048).rearrange("p (n g e) -> p n g e", n=TB, g=8)
        a_tmp = off(7680, 2048).rearrange("p (n g e) -> p n g e", n=TB, g=8)
        cmb = off(9728, 5 * 2 * 32).rearrange("p (x s n g) -> p x s n g", x=5, s=2, n=TB)
        sgb = off(13856, 2048).rearrange("p (m t) -> p m t", m=4)
        x1 = off(0, 4096).rearrange("p (n c) -> p n c", n=TB)
        xn2 = off(4096, 4096).rearrange("p (n c) -> p n c", n=TB)
        s_raw = off(8192, FT * SEQ).rearrange("p (m t) -> p m t", m=FT)
        sg = off(19456, 1024).rearrange("p (m t) -> p m t", m=2)
        y_out = off(4096, 4096).rearrange("p (n c) -> p n c", n=TB)

        ps = ctx.enter_context(nc.psum_tensor("ps", [P, 8, 512], F32))

        z_d = nc.dram_tensor("z_d", (9, SEQ, AW), F32, kind="Internal").ap()
        u_d = nc.dram_tensor("u_d", (NG * CH, CL, NC), F32, kind="Internal").ap()
        k_d = nc.dram_tensor("k_d", (NG, CH, CL * CH), F32, kind="Internal").ap()
        y_d = nc.dram_tensor("y_d", (NG * CH, CL, NC), F32, kind="Internal").ap()
        o_d = nc.dram_tensor("o_d", (2, NPAIR, SEQ, 2 * OW), F32, kind="Internal").ap()

        raw_landed = [sem(f"raw_landed{s}") for s in range(WRAW)]
        w_hi_done, w_lo_done = sem("w_hi_done"), sem("w_lo_done")
        gemm_steps = sem("gemm_steps")
        act_evac, dve_evac = sem("act_evac"), sem("dve_evac")
        misc_act, misc_dve = sem("misc_act"), sem("misc_dve")
        params_in, dsk_in = sem("params_in"), sem("dsk_in")
        x_loaded = [sem(f"x_loaded{n}") for n in range(TB)]
        first_in = sem("first_in")
        act_tab, dve_tab, pool_tab = sem("act_tab"), sem("dve_tab"), sem("pool_tab")
        sumsq_done, row_r_done, xn_done = sem("sumsq_done"), sem("row_r_done"), sem("xn_done")
        x_turned, hT_hi_done, hT_lo_done = sem("x_turned"), sem("hT_hi_done"), sem("hT_lo_done")
        c_turned = sem("c_turned")
        u_stored, uc_loaded = sem("u_stored"), sem("uc_loaded")
        z_stored, z_sq, z_sum, z_scaled, z_step = sem("z_stored"), sem("z_sq"), sem("z_sum"), sem("z_scaled"), sem("z_step")
        z_root, z_newton = sem("z_root"), sem("z_newton")
        w1_filled, kall_done, kall_out = sem("w1_filled"), sem("kall_done"), sem("kall_out")
        k_stored, toep_in, xst_zeroed = sem("k_stored"), sem("toep_in"), sem("xst_zeroed")
        s_done, scan_step, xst_done, y_done = sem("s_done"), sem("scan_step"), sem("xst_done"), sem("y_done")
        y_stored, yT_in = sem("y_stored"), sem("yT_in")
        yT_hi_done, yT_lo_done = sem("yT_hi_done"), sem("yT_lo_done")
        zt_qk_in, zt_k_in, zt_v_in = sem("zt_qk_in"), sem("zt_k_in"), sem("zt_v_in")
        qk_turned, scores_done, prob_done, prob_turned, o_done = (
            sem("qk_turned"), sem("scores_done"), sem("prob_done"), sem("prob_turned"), sem("o_done"))
        o_stored, oall_in = [sem(f"o_stored{b}") for b in range(2)], sem("oall_in")
        cmb_dve, cmb_act, a_ready, a_turned, aT_hi_done, aT_lo_done = (
            sem("cmb_dve"), sem("cmb_act"), sem("a_ready"), sem("a_turned"), sem("aT_hi_done"), sem("aT_lo_done"))
        glu_done, mix_done, mix_hi_done, mix_lo_done = (
            sem("glu_done"), sem("mix_done"), sem("mix_hi_done"), sem("mix_lo_done"))
        x1_in = sem("x1_in")
        s_raw_done, s_hi_done, s_lo_done = sem("s_raw_done"), sem("s_hi_done"), sem("s_lo_done")
        down_done, out_done, out_stored = sem("down_done"), sem("out_done"), sem("out_stored")

        O_FREE = 16
        MA_C, MA_W1, MA_K, MA_Y = 2, 6, 7, 11
        MD_W1, MD_S = 4, 5
        MA_PAIR, MD_PAIR = 11, 19
        MA_ATT, MD_ATT = MA_Y + NPAIR * MA_PAIR, MD_S + NPAIR * MD_PAIR

        def ma_probT(u):
            return 3 + u + 1

        def md_scores(u):
            return 3 + u + 1 + max(0, u - 2)

        def md_out(u):
            return 3 + min(8, u + 3) + u + 1

        AE_U, DE_U = 2, 2
        AE_Z, DE_Z = AE_U + 18, DE_U + 18
        AE_G = AE_Z + 16
        AE_GLU, DE_GLU = AE_G + 8, DE_Z + 8
        DE_MIX = DE_GLU + 8
        DE_OUT = DE_MIX + 8
        AE_F = AE_GLU + 2 * FB

        def wait_apart(eng, *waits):
            values = [eng.to_reg(value) for _, value in waits]
            eng.wait_ge(params_in, PARAMS)
            for (s, _), value in zip(waits, values):
                eng.wait_ge(s, value)

        def store_z(eng, sec, par):
            eng.dma_start(z_d[bass.ds(sec, 1)].rearrange("s (m p) c -> p (s m) c", p=P),
                          zs[:, bass.ds(par, 1)].rearrange("p b m c -> p (b m) c")).then_inc(z_stored, 16)

        TAB = {}
        ctx.enter_context(nc.allow_non_contiguous_dma(reason="small parameters"))
        block = ctx.enter_context(nc.Block())

        def in_cols(cc):
            return lambda j, h: t["w_in"][bass.ds((2 * j + h) * P, P), bass.ds(cc * 512, 512)]

        def cols(w, c):
            return lambda j, h: w[(2 * j + h) * P:(2 * j + h + 1) * P, c * 512:(c + 1) * 512]

        @block.sync
        def _(sp):
            def load(w, j, src, slot=None):
                if not (isinstance(w, int) and w < WRAW):
                    sp.wait_ge(w_lo_done, w - WRAW + 1)
                for h in range(2):
                    sp.dma_start(w_raw[:, j % WRAW, h * 512:(h + 1) * 512], src(j, h)).then_inc(raw_landed[j % WRAW], 16)

            for n in range(TB):
                sp.dma_start(x_in[:, n], t["x"][0, n * P:(n + 1) * P, :]).then_inc(x_loaded[n], 16)
                if n == 0:
                    sp.dma_start(ident[:, :], t["ident"]).then_inc(first_in, 16)
                    sp.dma_start(gmixT[:, :], t["g_mix"].rearrange("o (k p) -> p (o k)", p=P)).then_inc(first_in, 16)
            for j in range(4):
                load(W_U + j, j, in_cols(9))
            pin = lambda dst, src: sp.dma_start(dst, src).then_inc(params_in, 16)
            by_state = lambda a: a.rearrange("o (q two) s -> (two s) (o q)", two=2)
            pin(sv[LR], by_state(t["lambda_re"]))
            pin(sv[LI], by_state(t["lambda_im"]))
            for h in range(2):
                pin(sv[DT][h * 64:(h + 1) * 64], t["log_dt"].rearrange("o (q two) -> two (o q)", two=2)[h:h + 1]
                    .to_broadcast([64, NPR]))
            for r, name in enumerate(("b_re", "b_im")):
                pin(bnat[:, r], t[name].rearrange("o (q two) s c -> (two s) (o q) c", two=2))
            for r, name in enumerate(("c_re", "c_im")):
                for h in range(2):
                    for two in range(2):
                        pin(cnat[:, r, h, two * 64:(two + 1) * 64],
                            t[name].rearrange("o (h q two) c s -> two (o h) q c s", h=2, two=2)[two, h])
            pin(masks[:, :], t["masks"])
            pin(eye16[:, :], t["eye16"])
            pin(gffnT[:, :], t["g_ffn"].rearrange("o (k p) -> p (o k)", p=P))
            for n, name in enumerate(("g_q", "g_k")):
                for h in range(2):
                    pin(gqk[h * 64:(h + 1) * 64, n:n + 1], t[name].rearrange("o e -> e o"))
            for j in range(4):
                load(W_V + j, j, in_cols(6))
            sp.wait_ge(act_evac, AE_U)
            sp.wait_ge(dve_evac, DE_U)
            sp.dma_start(u_d.rearrange("(m p) j c -> p m (j c)", p=P), uT).then_inc(u_stored, 16)
            sp.wait_ge(u_stored, 16)
            ug = u_d.rearrange("(g h) j c -> h g j c", h=CH)
            for j in range(CL):
                sp.dma_start(uc[(CL - 1 - j) * CH:(CL - j) * CH], ug[:, :, j, :]).then_inc(uc_loaded, 16)
            with sp.Fori(1, 3) as c:
                for j in range(4):
                    load(W_V + 4 * c + j, j, in_cols(c + 6))
                sp.wait_ge(act_evac, AE_U + 2 * c)
                sp.wait_ge(dve_evac, DE_U + 2 * c)
                store_z(sp, c + 5, (c + 1) % 2)
                wait_apart(sp, (z_stored, 16 * c))
            for j in range(4):
                load(W_QK + j, j, in_cols(0))
            sp.wait_ge(act_evac, AE_U + 6)
            sp.wait_ge(dve_evac, DE_U + 6)
            store_z(sp, 8, 0)
            sp.wait_ge(z_stored, 48)
            with sp.Fori(1, 6) as c:
                for j in range(4):
                    load(W_QK + 4 * c + j, j, in_cols(c))
            for j in range(4):
                load(W_GATE + j, j, in_cols(10))

            def load_rows(sec, dst, i, done):
                src = z_d[sec][:, bass.ds(i * P, P)]
                if sec % 3 == 0:
                    sp.dma_start(dst.rearrange("p (n c) -> p n c", n=TB), src.rearrange("(n p) c -> p n c", p=P)
                                 ).then_inc(done, 16)
                else:
                    v = src.rearrange("(m a b) c -> a m b c", a=4, b=4)
                    for b in range(4):
                        sp.dma_start(dst[:, b * P:(b + 1) * P], v[:, :, b]).then_inc(done, 16)

            def load_pair(i, sections):
                for s in sections:
                    load_rows(s, off(s * 512, 512), i, zt_qk_in if s < 4 else zt_k_in)

            def load_values(i):
                for g in range(3):
                    load_rows(6 + g, late[:, bass.ds((i % 2) * V_STEP + (V_AT + g * 512), 512)], i, zt_v_in)

            sp.wait_ge(z_stored, 16 * 8)
            load_pair(0, range(5))
            sp.wait_ge(z_stored, 16 * 9)
            load_pair(0, (5,))
            load_values(0)
            sp.wait_ge(y_stored, 16 * (CL - 2))
            for b in range(2):
                sp.wait_ge(o_stored[b], O_FREE)
            with sp.Fori(1, NPAIR) as i:
                load(W_GATE + 4 * i, 0, in_cols(i + 10))
                sp.wait_ge(qk_turned, 6 * i)
                load_pair(i, range(6))
                load(W_GATE + 4 * i + 1, 1, in_cols(i + 10))
                sp.wait_ge(o_done, 8 * i - 7)
                load_values(i)
                for j in range(2, 4):
                    load(W_GATE + 4 * i + j, j, in_cols(i + 10))
            w = W_MIX
            for mat, c in (("b", 0), ("a", 0), ("b", 1), ("a", 1), ("p", 0), ("p", 1)):
                src = t[{"b": "w_glu_b", "a": "w_glu_a", "p": "w_attn_proj"}[mat]]
                for j in range(2):
                    sp.wait_ge(w_lo_done, w - WRAW + 1)
                    for h in range(2):
                        sp.dma_start(w_raw[:, w % WRAW, h * 512:(h + 1) * 512],
                                     cols(src, c)(j, h)).then_inc(raw_landed[w % WRAW], 16)
                    w += 1
            for c in range(2):
                for j in range(4):
                    load(W_OUT + 4 * c + j, j, cols(t["w_out"], c))
                if c == 0:
                    sp.wait_ge(a_ready, 1)
                    sp.dma_start(x1, t["x"].rearrange("b (n p) c -> p (b n) c", p=P)).then_inc(x1_in, 16)
            with sp.Fori(0, FB) as f:
                for j in range(4):
                    sp.wait_ge(w_lo_done, W_FFN - WRAW + 1 + j + 4 * f)
                    for h, name in enumerate(("w_ffn_gate", "w_ffn_up")):
                        sp.dma_start(w_raw[:, j, h * 512:(h + 1) * 512].rearrange("p (k c) -> p k c", k=2),
                                     t[name][2 * j * P:(2 * j + 2) * P, bass.ds(f * 256, 256)]
                                     .rearrange("(k p) c -> p k c", p=P)).then_inc(raw_landed[j], 16)

            def down(w, j, row):
                sp.wait_ge(w_lo_done, w - WRAW + 1)
                for h in range(2):
                    sp.dma_start(w_raw[:, j, h * 512:(h + 1) * 512],
                                 t["w_ffn_down"][bass.ds(row * P, P), h * 512:(h + 1) * 512]).then_inc(raw_landed[j], 16)

            with sp.Fori(0, FT // 4) as q:
                for j in range(4):
                    down(W_DOWN + j + 4 * q, j, q * 4 + j)
            for j in range(FT % 4):
                down(W_DOWN + FT // 4 * 4 + j, j, FT // 4 * 4 + j)
            for n in range(TB):
                sp.wait_ge(out_done, 2 * (n + 1))
                sp.dma_start(t["out"][0, n * P:(n + 1) * P, :], y_out[:, n]).then_inc(out_stored, 16)
            sp.wait_ge(out_stored, 16 * TB)

        @block.gpsimd
        def _(pool):
            n_tab = [0]

            def tab(ins):
                n_tab[0] += 1
                ins.then_inc(pool_tab, 1)
                pool.wait_ge(pool_tab, n_tab[0])

            def tt(out, a, b, op):
                tab(pool.tensor_tensor(out, a, b, op))

            def cmul(out_r, out_i, ar, ai, br, bi, tmp):
                tt(out_r, ar, br, ALU.mult)
                tt(tmp, ai, bi, ALU.mult)
                tt(out_r, out_r, tmp, ALU.subtract)
                tt(out_i, ar, bi, ALU.mult)
                tt(tmp, ai, br, ALU.mult)
                tt(out_i, out_i, tmp, ALU.add)

            tab(pool.memset(minus_half[:, :], -0.5))
            def row_root(n):
                ss = row_ss[:, n:n + 1]
                tab(pool.tensor_scalar(ss, ss, 1.0 / DM, EPS, ALU.mult, ALU.add))
                pool.tensor_tensor(row_r[:, n:n + 1], ss, minus_half[:, 0:1], ALU.pow).then_inc(row_r_done, 1)

            for n in range(TB):
                pool.wait_ge(sumsq_done, n + 1)
                row_root(n)
            tab(pool.memset(dsk, 0.0))
            d4 = t["d_skip"].rearrange("o (r q h c) -> q c h (o r)", r=4, q=4, h=2)
            for q in range(4):
                for h in range(2):
                    at = 32 * q + CH * h
                    pool.dma_start(dsk[at:at + CH, :], d4[q, :, h, :]).then_inc(dsk_in, 16)
            tab(pool.memset(toep_f, 0.0))
            tab(pool.memset(bb_f, 0.0))
            pool.wait_ge(act_tab, 5)
            pool.wait_ge(dve_tab, 14)
            pool.wait_ge(params_in, PARAMS)
            tt(sv[COS], sv[S2], sv[S2], ALU.mult)
            tab(pool.tensor_scalar(sv[COS], sv[COS], -2.0, 1.0, ALU.mult, ALU.add))
            tab(pool.memset(apw[:, 0, 0, :], 1.0))
            tab(pool.memset(apw[:, 1, 0, :], 0.0))
            tt(apw[:, 0, 1, :], sv[MAG], sv[COS], ALU.mult)
            tt(apw[:, 1, 1, :], sv[MAG], sv[SIN], ALU.mult)
            tab(pool.tensor_scalar(sv[NR], apw[:, 0, 1, :], -1.0, None, ALU.add))
            tt(sv[T1], sv[NR], sv[LR], ALU.mult)
            tt(sv[T2], apw[:, 1, 1, :], sv[LI], ALU.mult)
            tt(sv[T1], sv[T1], sv[T2], ALU.add)
            tt(sv[CR], sv[T1], sv[RD], ALU.mult)
            tt(sv[T1], apw[:, 1, 1, :], sv[LR], ALU.mult)
            tt(sv[T2], sv[NR], sv[LI], ALU.mult)
            tt(sv[T1], sv[T1], sv[T2], ALU.subtract)
            tt(sv[CI], sv[T1], sv[RD], ALU.mult)
            over_ch = lambda a: a.unsqueeze(2).to_broadcast([P, NPR, CH])
            cmul(bb[:, 0, 0:NPR, :], bb[:, 1, 0:NPR, :], bnat[:, 0], bnat[:, 1], over_ch(sv[CR]), over_ch(sv[CI]),
                 zsq[:, 0:NPR * CH].rearrange("p (q c) -> p q c", q=NPR))
            for k, n in ((1, 1), (2, 2), (4, 4)):
                at_k = lambda r: apw[:, r, k:k + 1, :].to_broadcast([P, n, NPR])
                cmul(apw[:, 0, k + 1:k + 1 + n, :], apw[:, 1, k + 1:k + 1 + n, :],
                     apw[:, 0, 1:1 + n, :], apw[:, 1, 1:1 + n, :], at_k(0), at_k(1),
                     zsq[:, 0:n * NPR].rearrange("p (k q) -> p k q", k=n))
            tab(pool.tensor_scalar(apn, apw[:, 1], -1.0, None, ALU.mult))
            for_k = lambda a, n: a[:, 0:n, :].rearrange("p k q -> p q k").unsqueeze(3).to_broadcast([P, NPR, n, CH])
            for_c = lambda a, n: a.unsqueeze(2).to_broadcast([P, NPR, n, CH])
            tmp = lambda n: zsq[:, 0:NPR * n * CH].rearrange("p (q k c) -> p q k c", q=NPR, k=n)
            cmul(aB[:, 0], aB[:, 1], for_k(apw[:, 0], CL), for_k(apw[:, 1], CL),
                 for_c(bb[:, 0, 0:NPR], CL), for_c(bb[:, 1, 0:NPR], CL), tmp(CL))
            pool.wait_ge(misc_act, MA_C)
            cmul(ca[:, 0], ca[:, 1], for_k(apw[:, 0], CL + 1), for_k(apn, CL + 1),
                 for_c(ctr[:, 0], CL + 1), for_c(ctr[:, 1], CL + 1), tmp(CL + 1))
            tab(pool.memset(bb2, 0.0))
            for h in range(2):
                rows = slice(64 * h, 64 * h + 64)
                tab(pool.tensor_copy(bb2[rows, :, :, h, :], bb[rows, :, 0:NPR, :]))
            TAB["ca"] = n_tab[0]
            small = sv[T1]
            cmul(sv[ER], sv[EI], sv[COS], sv[SIN], sv[COS], sv[SIN], small)
            cmul(sv[FR], sv[FI], sv[ER], sv[EI], sv[ER], sv[EI], small)
            cmul(sv[ER], sv[EI], sv[FR], sv[FI], sv[FR], sv[FI], small)
            tab(pool.memset(rot[:, 0, :, 0:1], 1.0))
            tab(pool.memset(rot[:, 1, :, 0:1], 0.0))
            n = 1
            while n < NC:
                by = lambda a: a.unsqueeze(2).to_broadcast([P, NPR, n])
                cmul(rot[:, 0, :, n:2 * n], rot[:, 1, :, n:2 * n], rot[:, 0, :, 0:n], rot[:, 1, :, 0:n],
                     by(sv[ER]), by(sv[EI]), spare[:, 0:NPR * n].rearrange("p (q c) -> p q c", q=NPR))
                cmul(sv[FR], sv[FI], sv[ER], sv[EI], sv[ER], sv[EI], small)
                tab(pool.tensor_copy(sv[ER], sv[FR]))
                tab(pool.tensor_copy(sv[EI], sv[FI]))
                n *= 2
            tab(pool.tensor_copy(m8row, sv[M8].unsqueeze(2).to_broadcast([P, NPR, NC])))
            tab(pool.memset(m8row[:, :, 0:1], 0.0))
            TAB["all"] = n_tab[0]

            pool.wait_ge(kall_out, 1)
            for q in range(4):
                pool.dma_start(k_d.rearrange("(r q h) c x -> q (h c) r x", r=4, q=4)[q],
                               kall[32 * q:32 * q + 32]).then_inc(k_stored, 16)
            pool.wait_ge(k_stored, 64)
            kg = k_d.rearrange("g c x -> c g x")
            for j in range(CL):
                n = (j + 1) * CH
                pool.dma_start(toep[j * CH:(j + 1) * CH, :, CL * CH - n:CL * CH], kg[:, :, 0:n]).then_inc(toep_in, 16)

            pool.wait_ge(s_done, 1)
            pool.memset(xst, 0.0).then_inc(xst_zeroed, 1)

            def store_o(i, b):
                dst = o_d[0][bass.ds(i, 1)].rearrange("i (n p) x -> p (i n) x", p=P)
                pool.dma_start(dst, ost[b][:, 0].rearrange("p n h e -> p n (h e)")).then_inc(o_stored[b], 16)
                dst = o_d[1][bass.ds(i, 1)].rearrange("i (m a b) x -> (i a) m b x", a=4, b=4)
                src = ost[b][:, 1].rearrange("p n h e -> p n (h e)")
                for c in range(4):
                    pool.dma_start(dst[:, :, c], src[:, c]).then_inc(o_stored[b], 16)

            pool.wait_ge(misc_act, MA_Y)
            for i in range(CL):
                pool.dma_start(y_d.rearrange("(q h c) i k -> i c q h k", q=NPR, h=2)[i],
                               rot_f.rearrange("p (q h c) -> p q h c", q=NPR, h=2)[i * CH:(i + 1) * CH]
                               ).then_inc(o_stored[i] if i < 2 else y_stored, 16)
            for b in range(2):
                pool.wait_ge(o_stored[b], O_FREE)
            pool.wait_ge(y_stored, 16 * (CL - 2))
            for b in range(2):
                pool.dma_start(yT_raw[:, 2 * b:2 * b + 2], y_d.rearrange("(m p) i k -> p m (i k)", p=P)[:, 2 * b:2 * b + 2]
                               ).then_inc(yT_in, 16)
            with pool.Fori(0, NPAIR // 2) as i2:
                for b in range(2):
                    i = i2 * 2 + b
                    pool.wait_ge(misc_dve, MD_S + MD_PAIR + MD_PAIR * i)
                    store_o(i, b)
            for b in range(2):
                pool.wait_ge(o_stored[b], O_FREE + 80 * NPAIR // 2)
            for s in range(2):
                for n in range(TB):
                    pool.dma_start(oall_d[:, s, n], o_d[s][:, n * P:(n + 1) * P, :].rearrange("i p x -> p i x")
                                   ).then_inc(oall_in, 16)
            for c in range(2):
                for m in range(4):
                    pool.wait_ge(dve_evac, DE_Z + 4 * c + m + 1)
                    g = gate[:, 8 + 4 * c + m]
                    pool.tensor_tensor(g, g, sgb[:, m], ALU.mult).then_inc(glu_done, 1)
            for n in range(TB):
                pool.wait_ge(sumsq_done, 2 * TB + n + 1)
                tt(row_ss[:, n:n + 1], row_ss[:, n:n + 1], row_ss2[:, n:n + 1], ALU.add)
                row_root(n)

        def rounder(act):
            def hi(w, j):
                act.wait_ge(raw_landed[j % WRAW], (w - j % WRAW) // WRAW * 32 + 32 if isinstance(w, int)
                            else 8 * (w - j % WRAW) + 32)
                if not (isinstance(w, int) and w < WSPL):
                    act.wait_ge(gemm_steps, 4 * w - 4)
                nc.scalar.activation(w_hi[:, j % WSPL], w_raw[:, j % WRAW], ACT.Copy).then_inc(w_hi_done, 1)
            return hi

        def subtracter(dve):
            def lo(w, j):
                dve.wait_ge(w_hi_done, w + 1)
                nc.vector.tensor_tensor(w_lo[:, j % WSPL], w_raw[:, j % WRAW], w_hi[:, j % WSPL].bitcast(F32),
                                        ALU.subtract).then_inc(w_lo_done, 1)
            return lo

        @block.scalar
        def _(act):
            hi = rounder(act)

            def evac(out, m, w_last, func=ACT.Copy):
                act.wait_ge(gemm_steps, 4 * w_last + m + 1)
                nc.scalar.activation(out, ps[:, m], func).then_inc(act_evac, 1)

            for n in range(TB):
                act.wait_ge(x_loaded[n], 16)
                nc.scalar.activation(zs[:, n // 2, 2 * (n % 2):2 * (n % 2) + 2].rearrange("p a b -> p (a b)"),
                                     x_in[:, n], ACT.Square, accum_out=row_ss[:, n:n + 1]).then_inc(sumsq_done, 1)
            hi(0, 0)

            def gained(wave, g):
                for k in range(KT):
                    act.wait_ge(x_turned, KT * wave + k + 1)
                    nc.scalar.activation(hT_hi[:, k], ps[:, k], ACT.Copy, scale=g[:, k:k + 1]).then_inc(hT_hi_done, 1)

            act.wait_ge(first_in, 32)
            gained(0, gmixT)
            hi(W_U + 1, 1)
            act.wait_ge(params_in, PARAMS)
            nc.scalar.activation(sv[DT], sv[DT], ACT.Exp).then_inc(act_tab, 1)
            act.wait_ge(dve_tab, 2)
            nc.scalar.activation(sv[MAG], sv[ZR], ACT.Exp).then_inc(act_tab, 1)
            nc.scalar.activation(sv[M8], sv[ZR], ACT.Exp, scale=float(CL)).then_inc(act_tab, 1)
            hi(W_U + 2, 2)
            act.wait_ge(dve_tab, 10)
            nc.scalar.activation(sv[SIN], sv[RR], ACT.Sin).then_inc(act_tab, 1)
            nc.scalar.activation(sv[S2], sv[RR], ACT.Sin, scale=0.5).then_inc(act_tab, 1)
            hi(W_U + 3, 3)
            hi(W_U + 4, 4)
            act.wait_ge(c_turned, 1)
            nc.scalar.activation(ctr_f[:, 0:256], ps[:, 4, 0:256], ACT.Copy).then_inc(misc_act, 1)
            nc.scalar.activation(ctr_f[:, 256:512], ps[:, 5, 0:256], ACT.Copy, scale=-1.0).then_inc(misc_act, 1)
            for m in (0, 2):
                act.wait_ge(gemm_steps, 4 * (W_V - 1) + m + 1)
                nc.scalar.activation(uT[:, m].rearrange("p (j c) -> p j c", j=CL),
                                     ps[:, m].rearrange("p (c j) -> p j c", j=CL), ACT.Copy).then_inc(act_evac, 1)

            def z_squares(c):
                act.wait_ge(act_evac, AE_Z - 10 + 2 * c)
                act.wait_ge(dve_evac, DE_Z - 10 + 2 * c)
                if not isinstance(c, int) or c > 0:
                    wait_apart(act, (z_sum, c))
                zc = zs[:, bass.ds((c + 1) % 2, 1)].rearrange("p b m c -> p (b m c)")
                nc.scalar.activation(zsq[:, 0:2048], zc, ACT.Square).then_inc(z_sq, 1)

            def z_roots(c):
                wait_apart(act, (z_sum, c + 1))
                nc.scalar.activation(z_r, z_r, ACT.Sqrt).then_inc(z_root, 1)

            def z_leaves(c):
                wait_apart(act, (z_stored, 16 * c + 48), (z_scaled, c + 1))
                store_z(act, c, (c + 1) % 2)

            def z_chunk(w0, c, first):
                hi(w0 + 4 * c + 1, 1)
                if not first:
                    z_squares(c - 1)
                hi(w0 + 4 * c + 2, 2)
                hi(w0 + 4 * c + 3, 3)
                if not first:
                    z_roots(c - 1)
                hi(w0 + 4 * c + 4, 4)
                if first:
                    act.wait_ge(z_stored, 32)
                else:
                    z_leaves(c - 1)
                for m in (0, 2):
                    evac(zs[:, bass.ds((c + 1) % 2, 1), m].rearrange("p b c -> p (b c)"), m, w0 + 4 * c + 3)

            for c in range(2):
                for j in range(1, 5):
                    hi(W_V + 4 * c + j, j)
                for m in (0, 2):
                    evac(zs[:, c, m], m, W_V + 4 * c + 3)
            for j in range(1, 5):
                hi(W_V + 8 + j, j)
            act.wait_ge(z_stored, 16)
            for m in (0, 2):
                evac(zs[:, 0, m], m, W_V + 11)
            act.wait_ge(uc_loaded, 16 * CL)
            for f in (0, 2, 4, 6):
                act.wait_ge(w1_filled, f + 1)
                nc.scalar.activation(w1T[:, f // 4, f % 4 * 4:f % 4 * 4 + 4].rearrange("p q x -> p (q x)"),
                                     ps[:, 4 + f % 4], ACT.Copy).then_inc(misc_act, 1)
            act.wait_ge(kall_done, 1)
            nc.scalar.activation(kall_f[:, 0:512], ps[:, 4], ACT.Copy).then_inc(misc_act, 1)
            z_chunk(W_QK, 0, True)
            act.wait_ge(pool_tab, TAB["ca"])
            with act.Fori(1, 6) as c:
                z_chunk(W_QK, c, False)
            z_squares(5)
            z_roots(5)
            z_leaves(5)
            for b in range(4):
                act.wait_ge(y_done, b + 1)
                nc.scalar.activation(ygelu[:, b * 512:(b + 1) * 512], ps[:, 4 + b], ACT.Gelu_apprx_tanh
                                     ).then_inc(misc_act, 1)

            with act.Fori(0, NPAIR // 2) as i2:
                for b in range(2):
                    i = i2 * 2 + b
                    hi(W_GATE + 1 + 4 * i, 1)
                    for g in range(3):
                        act.wait_ge(qk_turned, 6 * i + g + 1)
                        nc.scalar.activation(qT[:, g], ps[:, 4 + g], ACT.Copy, scale=gqk[:, 2:3]).then_inc(misc_act, 1)
                    for u in range(9):
                        if u < 8:
                            act.wait_ge(misc_dve, MD_S + md_scores(u) + MD_PAIR * i)
                            n, h = u // 2, u % 2
                            if u >= 2:
                                act.wait_ge(prob_turned, 8 * i + u - 1)
                            k0 = 0 if n else P
                            nc.scalar.activation(prob[:, u % 2, k0:256], negs[:, u % 2, k0:256], ACT.Exp, scale=-1.0,
                                                 bias=ost[b][:, 0, n, h, HD:HD + 1],
                                                 accum_out=ost[b][:, 0, n, h, HD + 1:HD + 2])
                            nc.scalar.activation(prob[:, u % 2, 256:512], negs[:, u % 2, 256:512], ACT.Exp, scale=-1.0,
                                                 bias=ost[b][:, 1, n, h, HD:HD + 1],
                                                 accum_out=ost[b][:, 1, n, h, HD + 1:HD + 2]).then_inc(prob_done, 1)
                        if u == 5:
                            act.wait_ge(yT_in, 32)
                            nc.scalar.activation(yT_hi[:, bass.ds(i, 1)].rearrange("p m (c i) -> p (m c) i", i=CL),
                                                 yT_raw[:, bass.ds(i, 1)].rearrange("p m (i c) -> p (m c) i", i=CL),
                                                 ACT.Copy).then_inc(yT_hi_done, 1)
                        if u >= 1:
                            v = u - 1
                            k0 = 0 if v // 2 else P
                            act.wait_ge(prob_turned, 8 * i + v + 1)
                            if v >= 2:
                                act.wait_ge(o_done, 8 * i + v - 1)
                            nc.scalar.activation(probT[:, v % 2, k0:512], ps[:, 6, k0:512], ACT.Copy).then_inc(misc_act, 1)
                        if u in (1, 4, 7):
                            hi(W_GATE + u // 3 + 2 + 4 * i, u // 3 + 2)
                    for m in range(4):
                        evac(gate[:, bass.ds(i * 4 + m, 1)].rearrange("p b c -> p (b c)"), m, W_GATE + 3 + 4 * i, ACT.Sigmoid)

            w = W_MIX
            for c in range(2):
                hi(w + 1, w + 1)
                if c:
                    act.wait_ge(cmb_dve, 3)
                    nc.scalar.activation(cmb[:, 1], cmb[:, 0], ACT.Exp).then_inc(cmb_act, 1)
                hi(w + 2, w + 2)
                if c:
                    act.wait_ge(glu_done, 4)
                for m in range(4):
                    evac(sgb[:, m], m, w + 1, ACT.Sigmoid)
                hi(w + 3, w + 3)
                hi(w + 4, w + 4)
                w += 4
            for k in range(4):
                act.wait_ge(a_turned, k + 1)
                nc.scalar.activation(aT_hi[:, k], ps[:, 4 + k], ACT.Copy).then_inc(aT_hi_done, 1)
            for c in range(2):
                hi(w + 1, w + 1)
                hi(w + 2, w + 2)
                for m in range(4):
                    act.wait_ge(mix_done, 4 * c + m + 1)
                    nc.scalar.activation(hT_hi[:, 4 * c + m], gate[:, 4 * c + m], ACT.Copy).then_inc(mix_hi_done, 1)
                w += 2

            def half_squares(c, sums):
                for n in range(TB):
                    act.wait_ge(dve_evac, DE_MIX + 4 * c + n + 1)
                    at = slice(c * 512, (c + 1) * 512)
                    nc.scalar.activation(xn2[:, n, at], x1[:, n, at], ACT.Square, accum_out=sums[:, n:n + 1]
                                         ).then_inc(sumsq_done, 1)

            for j in range(1, 6):
                hi(W_OUT + j, j)
            half_squares(0, row_ss)
            for j in range(6, 9):
                hi(W_OUT + j, j)
            half_squares(1, row_ss2)
            gained(1, gffnT)
            with act.Fori(0, FB) as f:
                for j in range(1, 5):
                    hi(W_FFN + j + 4 * f, j)
                for m in range(2):
                    act.wait_ge(s_raw_done, 2 * f + m + 1)
                    evac(sg[:, m], m, W_FFN + 3 + 4 * f, ACT.Silu)

            def s_hi(row, j, q):
                act.wait_ge(gemm_steps, 4 * (W_DOWN + j - 1) + 4 * q)
                nc.scalar.activation(yT_hi[:, j % 2], s_raw[:, bass.ds(row, 1)].rearrange("p b c -> p (b c)"),
                                     ACT.Copy).then_inc(s_hi_done, 1)

            act.wait_ge(s_raw_done, 3)
            s_hi(0, 0, 0)
            act.wait_ge(s_raw_done, 2 + 2 * FB)
            with act.Fori(0, FT // 4) as q:
                for j in range(1, 5):
                    hi(W_DOWN + j + 4 * q, j)
                    s_hi(q * 4 + j, j, 4 * q)
            hi(W_END - 1, 1)
            s_hi(FT - 1, 1, FT - 2)

        @block.vector
        def _(dve):
            lo = subtracter(dve)
            V = nc.vector
            n_tab = [0]

            def tab(ins):
                n_tab[0] += 1
                ins.then_inc(dve_tab, 1)
                dve.wait_ge(dve_tab, n_tab[0])

            def turn_lo(wave, g):
                for k in range(KT):
                    dve.wait_ge(hT_hi_done, KT * wave + k + 1)
                    V.scalar_tensor_tensor(out=hT_lo[:, k], in0=ps[:, k], scalar=g[:, k:k + 1],
                                           in1=hT_hi[:, k].bitcast(F32), op0=ALU.mult, op1=ALU.subtract
                                           ).then_inc(hT_lo_done, 1)

            def evac(out, m, w_last):
                dve.wait_ge(gemm_steps, 4 * w_last + m + 1)
                V.tensor_copy(out, ps[:, m]).then_inc(dve_evac, 1)

            for n in range(TB):
                dve.wait_ge(row_r_done, n + 1)
                V.tensor_scalar(x_in[:, n], x_in[:, n], row_r[:, n:n + 1], None, ALU.mult).then_inc(xn_done, 1)
            lo(0, 0)
            dve.wait_ge(first_in, 32)
            turn_lo(0, gmixT)
            lo(W_U + 1, 1)
            dve.wait_ge(act_tab, 1)
            tab(V.tensor_tensor(sv[ANG], sv[LI], sv[DT], ALU.mult))
            tab(V.tensor_tensor(sv[ZR], sv[LR], sv[DT], ALU.mult))
            lo(W_U + 2, 2)
            tab(V.tensor_scalar(sv[KQ], sv[ANG], 1.0 / TWO_PI, ROUND, ALU.mult, ALU.add))
            tab(V.tensor_scalar(sv[KQ], sv[KQ], -ROUND, None, ALU.add))
            tab(V.scalar_tensor_tensor(out=sv[RR], in0=sv[KQ], scalar=-C1, in1=sv[ANG], op0=ALU.mult, op1=ALU.add))
            tab(V.scalar_tensor_tensor(out=sv[RR], in0=sv[KQ], scalar=-C2, in1=sv[RR], op0=ALU.mult, op1=ALU.add))
            tab(V.scalar_tensor_tensor(out=sv[RR], in0=sv[KQ], scalar=-C3, in1=sv[RR], op0=ALU.mult, op1=ALU.add))
            tab(V.tensor_scalar(sv[RR], sv[RR], PI_BELOW, -PI_BELOW, ALU.min, ALU.max))
            tab(V.tensor_tensor(sv[DEN], sv[LR], sv[LR], ALU.mult))
            tab(V.tensor_tensor(sv[SQ], sv[LI], sv[LI], ALU.mult))
            tab(V.tensor_tensor(sv[DEN], sv[DEN], sv[SQ], ALU.add))
            tab(V.reciprocal(sv[RD], sv[DEN]))
            tab(V.tensor_tensor(gqk[:, 2:3], gqk[:, 0:1], gqk[:, 1:2], ALU.mult))
            tab(V.tensor_scalar(gqk[:, 2:3], gqk[:, 2:3], HD ** -0.5, None, ALU.mult))
            dve.wait_ge(dsk_in, 128)
            V.tensor_tensor(dadd, eye16[:, :].unsqueeze(1).to_broadcast([P, 4, CH]),
                            dsk.unsqueeze(2).to_broadcast([P, 4, CH]), ALU.mult).then_inc(dve_tab, 1)
            lo(W_U + 3, 3)
            lo(W_U + 4, 4)
            for m in (1, 3):
                dve.wait_ge(gemm_steps, 4 * (W_V - 1) + m + 1)
                V.tensor_copy(uT[:, m].rearrange("p (j c) -> p j c", j=CL),
                              ps[:, m].rearrange("p (c j) -> p j c", j=CL)).then_inc(dve_evac, 1)
            for c in range(2):
                for j in range(1, 5):
                    lo(W_V + 4 * c + j, j)
                for m in (1, 3):
                    evac(zs[:, c, m], m, W_V + 4 * c + 3)
            for j in range(1, 5):
                lo(W_V + 8 + j, j)
            dve.wait_ge(z_stored, 16)
            for m in (1, 3):
                evac(zs[:, 0, m], m, W_V + 11)
            dve.wait_ge(uc_loaded, 16 * CL)
            for f in (1, 3, 5, 7):
                dve.wait_ge(w1_filled, f + 1)
                V.tensor_copy(w1T[:, f // 4, f % 4 * 4:f % 4 * 4 + 4].rearrange("p q x -> p (q x)"),
                              ps[:, 4 + f % 4]).then_inc(misc_dve, 1)
            dve.wait_ge(dve_tab, n_tab[0] + 1)
            dve.wait_ge(misc_act, MA_K)
            kd = kall[:, :, 0:CH]
            V.tensor_tensor(kd, kd, dadd, ALU.add).then_inc(kall_out, 1)

            def z_sums(c):
                dve.wait_ge(z_sq, c + 1)
                V.tensor_reduce(z_ss, zsq[:, 0:2048].rearrange("p (g e) -> p g e", e=HD), AX_X, ALU.add).then_inc(z_step, 1)
                dve.wait_ge(z_step, 2 * c + 1)
                V.tensor_scalar(z_ss, z_ss, 1.0 / HD, EPS, ALU.mult, ALU.add).then_inc(z_step, 1)
                dve.wait_ge(z_step, 2 * c + 2)
                V.reciprocal(z_r, z_ss).then_inc(z_sum, 1)

            def z_scale(c):
                zh = zs[:, bass.ds((c + 1) % 2, 1)].rearrange("p b m (g e) -> p (b m g) e", e=HD)
                wait_apart(dve, (z_root, c + 1))
                V.tensor_tensor(z_t, z_r, z_r, ALU.mult).then_inc(z_newton, 1)
                dve.wait_ge(z_newton, 4 * c + 1)
                V.tensor_tensor(z_t, z_t, z_ss, ALU.mult).then_inc(z_newton, 1)
                dve.wait_ge(z_newton, 4 * c + 2)
                V.tensor_scalar(z_t, z_t, -0.5, 1.5, ALU.mult, ALU.add).then_inc(z_newton, 1)
                dve.wait_ge(z_newton, 4 * c + 3)
                V.tensor_tensor(z_r, z_r, z_t, ALU.mult).then_inc(z_newton, 1)
                dve.wait_ge(z_newton, 4 * c + 4)
                V.tensor_tensor(zh, zh, z_r.unsqueeze(2).to_broadcast([P, 32, HD]), ALU.mult).then_inc(z_scaled, 1)

            def z_chunk(c, first=False, also=()):
                lo(W_QK + 4 * c + 1, 1)
                for step in also[0:1]:
                    step()
                lo(W_QK + 4 * c + 2, 2)
                if not first:
                    z_sums(c - 1)
                lo(W_QK + 4 * c + 3, 3)
                if not first:
                    z_scale(c - 1)
                lo(W_QK + 4 * c + 4, 4)
                for step in also[1:2]:
                    step()
                dve.wait_ge(z_stored, 16 * c + 32)
                for m in (1, 3):
                    evac(zs[:, bass.ds((c + 1) % 2, 1), m].rearrange("p b c -> p (b c)"), m, W_QK + 4 * c + 3)

            z_chunk(0, True)
            with dve.Fori(1, 3) as c:
                z_chunk(c)

            n_scan = [0]

            def scan(ins, sync=True):
                n_scan[0] += 1
                ins.then_inc(scan_step, 1)
                if sync:
                    dve.wait_ge(scan_step, n_scan[0])

            s_re = ps[:, 4:6, :].rearrange("p b x -> p (b x)")
            s_im = ps[:, 6:8, :].rearrange("p b x -> p (b x)")
            r_re, r_im = rot_f[:, 0:1024], rot_f[:, 1024:2048]
            tmp = kall_f
            zr, zi, yr, yi = turned
            grid = lambda a: a.rearrange("p (q c) -> p q c", q=NPR)
            cut_c = lambda a: grid(a)[:, :, 0:NC - 1]

            def to_states(r, half_step, op):
                for h in range(2):
                    rows = slice(64 * h, 64 * h + 64)
                    ins = V.tensor_tensor(xst[rows, r, :, h, 1:NC], cut_c(turned[r])[rows], cut_c(tmp)[rows], op)
                    if r == 0 or h == 0:
                        half_step(ins)
                    else:
                        ins.then_inc(xst_done, 1)

            def turn_re():
                dve.wait_ge(s_done, 1)
                dve.wait_ge(pool_tab, TAB["all"])
                dve.wait_ge(k_stored, 64)
                scan(V.tensor_tensor(zr, s_re, r_re, ALU.mult), False)
                scan(V.tensor_tensor(tmp, s_im, r_im, ALU.mult))
                scan(V.tensor_tensor(zr, zr, tmp, ALU.add))

            def turn_im():
                scan(V.tensor_tensor(zi, s_im, r_re, ALU.mult), False)
                V.tensor_tensor(tmp, s_re, r_im, ALU.mult).then_inc(misc_dve, 1)
                dve.wait_ge(misc_dve, MD_S)
                dve.wait_ge(scan_step, n_scan[0])
                scan(V.tensor_tensor(zi, zi, tmp, ALU.subtract))

            def scan_re():
                scan(V.tensor_tensor_scan(yr, m8row_f, zr, 0.0, ALU.mult, ALU.add))

            def scan_im():
                scan(V.tensor_tensor_scan(yi, m8row_f, zi, 0.0, ALU.mult, ALU.add))

            def back_re():
                dve.wait_ge(xst_zeroed, 1)
                scan(V.tensor_tensor(cut_c(zr), cut_c(yr), cut_c(r_re), ALU.mult), False)
                scan(V.tensor_tensor(cut_c(tmp), cut_c(yi), cut_c(r_im), ALU.mult))
                to_states(0, scan, ALU.subtract)

            def back_im():
                scan(V.tensor_tensor(cut_c(zi), cut_c(yi), cut_c(r_re), ALU.mult), False)
                scan(V.tensor_tensor(cut_c(tmp), cut_c(yr), cut_c(r_im), ALU.mult))
                to_states(1, scan, ALU.add)

            z_chunk(3, also=(turn_re, turn_im))
            z_chunk(4, also=(scan_re, scan_im))
            z_chunk(5, also=(back_re, back_im))
            z_sums(5)
            z_scale(5)

            def add_o(u, b):
                n, h = u // 2, u % 2
                return V.tensor_copy(ost[b][:, :, n, h, 0:HD],
                                     ps[:, 7, (u % 4) * P:(u % 4 + 1) * P].rearrange("p (s e) -> p s e", s=2)
                                     ).then_inc(misc_dve, 1)

            with dve.Fori(0, NPAIR // 2) as i2:
                for b in range(2):
                    i = i2 * 2 + b
                    lo(W_GATE + 1 + 4 * i, 1)
                    for g in range(3):
                        dve.wait_ge(qk_turned, 6 * i + g + 4)
                        V.tensor_copy(kT[:, g], ps[:, 4 + (3 + g) % 4]).then_inc(misc_dve, 1)
                    for u in range(10):
                        if u == 0:
                            dve.wait_ge(o_stored[b], 80 * i2 + O_FREE)
                        if u < 8:
                            n, h = u // 2, u % 2
                            wait_apart(dve, (scores_done, 8 * i + u + 1),
                                       *([(prob_done, 8 * i + u - 1)] if u >= 2 else []))
                            k0 = 0 if n else P
                            V.tensor_tensor_reduce(negs[:, u % 2, k0:256], ps[:, 4 + u % 2, k0:256], masks[:, k0:256],
                                                   -1.0, 3.0e38, ALU.add, ALU.min, ost[b][:, 0, n, h, HD:HD + 1])
                            V.tensor_tensor_reduce(negs[:, u % 2, 256:512], ps[:, 4 + u % 2, 256:512], masks[:, 256:512],
                                                   -1.0, 3.0e38, ALU.add, ALU.min, ost[b][:, 1, n, h, HD:HD + 1]
                                                   ).then_inc(misc_dve, 1)
                        if u == 6:
                            wait_apart(dve, (yT_hi_done, i + 1))
                            V.tensor_tensor(yT_lo[:, bass.ds(i, 1)].rearrange("p m (c i) -> p (m c) i", i=CL),
                                            yT_raw[:, bass.ds(i, 1)].rearrange("p m (i c) -> p (m c) i", i=CL),
                                            yT_hi[:, bass.ds(i, 1)].bitcast(F32).rearrange("p m (c i) -> p (m c) i", i=CL),
                                            ALU.subtract).then_inc(yT_lo_done, 1)
                        if u >= 2:
                            dve.wait_ge(o_done, 8 * i + u - 1)
                            add_o(u - 2, b)
                        if u in (1, 4, 7):
                            lo(W_GATE + u // 3 + 2 + 4 * i, u // 3 + 2)

            n_cmb = [0]

            def step(ins, sync=True):
                n_cmb[0] += 1
                ins.then_inc(cmb_dve, 1)
                if sync:
                    dve.wait_ge(cmb_dve, n_cmb[0])

            stat = lambda s, e: oall[:, s, :, :, HD + e]
            wide = lambda a: a.unsqueeze(3).to_broadcast([P, TB, 8, HD])

            def combine():
                dve.wait_ge(oall_in, 128)
                step(V.tensor_tensor(cmb[:, 2, 0], stat(0, 0), stat(1, 0), ALU.min))
                for s in range(2):
                    step(V.tensor_tensor(cmb[:, 0, s], cmb[:, 2, 0], stat(s, 0), ALU.subtract), s == 1)
                dve.wait_ge(cmb_act, 1)
                for s in range(2):
                    step(V.tensor_tensor(cmb[:, 3, s], cmb[:, 1, s], stat(s, 1), ALU.mult), s == 1)
                step(V.tensor_tensor(cmb[:, 2, 0], cmb[:, 3, 0], cmb[:, 3, 1], ALU.add))
                step(V.reciprocal(cmb[:, 2, 1], cmb[:, 2, 0]))
                for s in range(2):
                    step(V.tensor_tensor(cmb[:, 4, s], cmb[:, 1, s], cmb[:, 2, 1], ALU.mult), s == 1)

            def combined():
                step(V.tensor_tensor(a_tok, oall[:, 0, :, :, 0:HD], wide(cmb[:, 4, 0]), ALU.mult), False)
                step(V.tensor_tensor(a_tmp, oall[:, 1, :, :, 0:HD], wide(cmb[:, 4, 1]), ALU.mult))
                V.tensor_tensor(a_tok, a_tok, a_tmp, ALU.add).then_inc(a_ready, 1)

            w = W_MIX
            for c in range(2):
                lo(w + 1, w + 1)
                if c:
                    combine()
                lo(w + 2, w + 2)
                if c:
                    combined()
                lo(w + 3, w + 3)
                lo(w + 4, w + 4)
                if c:
                    for k in range(4):
                        dve.wait_ge(aT_hi_done, k + 1)
                        V.tensor_tensor(aT_lo[:, k], ps[:, 4 + k], aT_hi[:, k].bitcast(F32), ALU.subtract
                                        ).then_inc(aT_lo_done, 1)
                for m in range(4):
                    dve.wait_ge(gemm_steps, 4 * (w + 3) + m + 1)
                    dve.wait_ge(act_evac, AE_G + 4 * c + m + 1)
                    V.tensor_tensor(sgb[:, m], sgb[:, m], ps[:, m], ALU.mult).then_inc(dve_evac, 1)
                w += 4
            for c in range(2):
                lo(w + 1, w + 1)
                lo(w + 2, w + 2)
                for m in range(4):
                    dve.wait_ge(gemm_steps, 4 * (w + 1) + m + 1)
                    ga = gate[:, 4 * c + m]
                    V.tensor_tensor(ga, ga, ps[:, m], ALU.mult).then_inc(dve_evac, 1)
                    dve.wait_ge(dve_evac, DE_GLU + 4 * c + m + 1)
                    dve.wait_ge(glu_done, 4 * c + m + 1)
                    V.tensor_tensor(ga, ga, gate[:, 8 + 4 * c + m], ALU.add).then_inc(mix_done, 1)
                for m in range(4):
                    dve.wait_ge(mix_hi_done, 4 * c + m + 1)
                    V.tensor_tensor(hT_lo[:, 4 * c + m], gate[:, 4 * c + m], hT_hi[:, 4 * c + m].bitcast(F32),
                                    ALU.subtract).then_inc(mix_lo_done, 1)
                w += 2
            def normalised(n):
                dve.wait_ge(row_r_done, TB + n + 1)
                V.tensor_scalar(xn2[:, n], x1[:, n], row_r[:, n:n + 1], None, ALU.mult).then_inc(xn_done, 1)

            dve.wait_ge(x1_in, 16)
            for c in range(2):
                for j in range(1, 5):
                    lo(W_OUT + 4 * c + j, j)
                for n in range(TB):
                    dve.wait_ge(gemm_steps, 4 * (W_OUT + 4 * c + 3) + n + 1)
                    xh = x1[:, n, c * 512:(c + 1) * 512]
                    V.tensor_tensor(xh, xh, ps[:, n], ALU.add).then_inc(dve_evac, 1)
                    if c and n == 2:
                        normalised(0)
            for n in range(1, TB):
                normalised(n)
            V.engine_nop().then_inc(s_raw_done, 1)
            V.engine_nop().then_inc(s_raw_done, 1)
            turn_lo(1, gffnT)
            with dve.Fori(0, FB) as f:
                for j in range(1, 5):
                    lo(W_FFN + j + 4 * f, j)
                for m in range(2):
                    dve.wait_ge(act_evac, AE_GLU + m + 1 + 2 * f)
                    dve.wait_ge(gemm_steps, 4 * (W_FFN + 3) + 2 + m + 1 + 16 * f)
                    V.tensor_tensor(s_raw[:, bass.ds(f * 2 + m, 1)].rearrange("p b c -> p (b c)"), sg[:, m],
                                    ps[:, 2 + m], ALU.mult).then_inc(s_raw_done, 1)

            def s_lo(row, j):
                dve.wait_ge(s_hi_done, row + 1)
                V.tensor_tensor(yT_lo[:, j % 2], s_raw[:, bass.ds(row, 1)].rearrange("p b c -> p (b c)"),
                                yT_hi[:, j % 2].bitcast(F32), ALU.subtract).then_inc(s_lo_done, 1)

            dve.wait_ge(s_raw_done, 2 + 2 * FB)
            s_lo(0, 0)
            with dve.Fori(0, FT // 4) as q:
                for j in range(1, 5):
                    lo(W_DOWN + j + 4 * q, j)
                    s_lo(q * 4 + j, j)
            lo(W_END - 1, 1)
            s_lo(FT - 1, 1)
            for m in range(2 * TB):
                dve.wait_ge(down_done, m + 1)
                at = slice(m % 2 * 512, (m % 2 + 1) * 512)
                V.tensor_tensor(y_out[:, m // 2, at], x1[:, m // 2, at], ps[:, m], ALU.add).then_inc(out_done, 1)

        @block.tensor
        def _(pe):
            T = nc.tensor

            def products(w, j, first, last, operands, bank_free, ready=None):
                for m in range(4):
                    if m == 0:
                        pe.wait_ge(w_lo_done, w + 1)
                    if first:
                        bank_free(m)
                    if ready:
                        ready(m)
                    for h in range(2):
                        for k, (a, b) in enumerate(((0, 0), (1, 0), (0, 1))):
                            lhsT, rhs = operands(m, h, (w_hi, w_lo)[b][:, j % WSPL, h * 512:(h + 1) * 512], a)
                            ins = T.matmul(ps[:, m], lhsT, rhs, start=first and h == 0 and k == 0,
                                           stop=last and h == 1 and k == 2)
                    ins.then_inc(gemm_steps, 1)
                    yield

            def by_token(acts, j):
                return lambda m, h, w, a: (acts[a][:, 2 * j + h, m * P:(m + 1) * P], w)

            def by_feature(acts, j):
                return lambda m, h, w, a: (w[:, m * P:(m + 1) * P], acts[a][:, 2 * j + h, :])

            def columns(w0, n, how, acts, bank_free, ready=None):
                for j in range(n):
                    jj = j if not isinstance(w0, int) else w0 + j
                    yield from products(w0 + j, jj, j == 0, j == n - 1, how(acts, j), bank_free,
                                        ready and (lambda m, j=j: ready(j, m)))

            def split_rows(done, base):
                def ready(j, m):
                    if m == 0:
                        pe.wait_ge(done, base + 2 * j + 2)
                return ready

            def turned_rows(base, j, m):
                if m == 0:
                    pe.wait_ge(hT_lo_done, base + 2 * j + 2)
                elif j == 0 and m >= 2:
                    pe.wait_ge(hT_lo_done, base + m + 1)

            def run(gen):
                for _ in gen:
                    pass

            h_acts, y_acts, a_acts = (hT_hi, hT_lo), (yT_hi, yT_lo), (aT_hi, aT_lo)

            def rows_turned(wave, src):
                for n in range(TB):
                    pe.wait_ge(xn_done, TB * wave + n + 1)
                    for k in range(KT):
                        ins = T.transpose(ps[:, k, n * P:(n + 1) * P], src[:, n, k * P:(k + 1) * P], ident[:, :])
                        if n == TB - 1:
                            ins.then_inc(x_turned, 1)

            pe.wait_ge(first_in, 32)
            rows_turned(0, x_in)
            ssm_in = columns(W_U, 4, by_feature, h_acts, lambda m: None, lambda j, m: turned_rows(0, j, m))
            for _ in range(12):
                next(ssm_in)
            pe.wait_ge(params_in, PARAMS)
            for r in range(2):
                for h in range(2):
                    ins = T.transpose(ps[:, 4 + r, h * P:(h + 1) * P], cnat[:, r, h], ident[:, :])
            ins.then_inc(c_turned, 1)
            run(ssm_in)

            def alternating(a0, d0):
                def free(m):
                    pe.wait_ge(act_evac if m % 2 == 0 else dve_evac, (a0 if m % 2 == 0 else d0) + m // 2 + 1)
                return free

            with pe.Fori(0, 3) as c:
                run(columns(W_V + 4 * c, 4, by_token, h_acts, alternating(2 * c, 2 * c)))

            pe.wait_ge(pool_tab, TAB["ca"])
            pe.wait_ge(misc_act, MA_C)
            for f in range(8):
                if f >= 4:
                    pe.wait_ge(misc_act if f % 2 == 0 else misc_dve, (MA_C if f % 2 == 0 else 0) + (f - 4) // 2 + 1)
                for x in range(4):
                    ins = T.transpose(ps[:, 4 + f % 4, x * P:(x + 1) * P],
                                      aB[:, f // 4, f % 4 * 4 + x].rearrange("p k c -> p (k c)"), ident[:, :])
                ins.then_inc(w1_filled, 1)
            pe.wait_ge(misc_act, MA_C + 3)
            for q in range(NPR):
                for r in range(2):
                    ins = T.matmul(ps[32 * (q % 4):32 * (q % 4) + 32, 4, q // 4 * P:(q // 4 + 1) * P],
                                   bb2[:, r, q].rearrange("p h c -> p (h c)"),
                                   ca[:, r, q, 0:CL].rearrange("p k c -> p (k c)"), start=r == 0, stop=r == 1)
            ins.then_inc(kall_done, 1)

            with pe.Fori(0, 3) as c:
                run(columns(W_QK + 4 * c, 4, by_token, h_acts, alternating(AE_U + 4 + 2 * c, DE_U + 4 + 2 * c)))
            pe.wait_ge(uc_loaded, 16 * CL)
            pe.wait_ge(misc_act, MA_K)
            pe.wait_ge(misc_dve, MD_W1)
            for r in range(2):
                for q in range(NPR):
                    for h in range(2):
                        ins = T.matmul(ps[64 * h:64 * h + 64, 4 + 2 * r + q // 8, q % 8 * NC:(q % 8 + 1) * NC],
                                       w1T[:, r, q, 64 * h:64 * h + 64], uc[:, 2 * q + h], start=True, stop=True)
            ins.then_inc(s_done, 1)
            with pe.Fori(3, 6) as c:
                run(columns(W_QK + 4 * c, 4, by_token, h_acts, alternating(AE_U + 4 + 2 * c, DE_U + 4 + 2 * c)))
            pe.wait_ge(xst_done, 1)
            pe.wait_ge(toep_in, 16 * CL)
            for q in range(NPR):
                out = ps[:, 4 + q // 4, q % 4 * 2 * NC:(q % 4 + 1) * 2 * NC]
                for r in range(2):
                    T.matmul(out, ca[:, r, q, 1:CL + 1].rearrange("p k c -> p (k c)"),
                             xst[:, r, q].rearrange("p h c -> p (h c)"), start=r == 0, stop=r == 1)
                for h in range(2):
                    ins = T.matmul(out[:, h * NC:(h + 1) * NC], toep[:, 2 * q + h], uc[:, 2 * q + h], start=False,
                                   stop=True, skip_group_check=True)
                if q % 4 == 3:
                    ins.then_inc(y_done, 1)

            def scores(i, u):
                n, h = u // 2, u % 2
                rows = slice(64 * h, 64 * h + 64)
                if u >= 2:
                    pe.wait_ge(misc_dve, MD_S + md_scores(u - 2) + MD_PAIR * i)
                k0 = 0 if n else P
                q = slice(n * P, (n + 1) * P)
                bank = 4 + u % 2
                T.matmul(ps[:, bank, k0:256], qT[rows, 0, q], kT[rows, 0, n * P - P + k0:n * P + P],
                         start=True, stop=True)
                for g in (1, 2):
                    ins = T.matmul(ps[:, bank, (g + 1) * P:(g + 2) * P], qT[rows, g, q], kT[rows, g, q],
                                   start=True, stop=True)
                ins.then_inc(scores_done, 1)

            def turn_prob(i, u):
                pe.wait_ge(prob_done, 8 * i + u + 1)
                if u:
                    pe.wait_ge(misc_act, MA_Y + ma_probT(u - 1) + MA_PAIR * i)
                for x in range(0 if u // 2 else 1, 4):
                    ins = T.transpose(ps[:, 6, x * P:(x + 1) * P], prob[:, u % 2, x * P:(x + 1) * P], ident[:, :])
                ins.then_inc(prob_turned, 1)

            def values(i, u, b):
                n, h = u // 2, u % 2
                pe.wait_ge(misc_act, MA_Y + ma_probT(u) + MA_PAIR * i)
                if u == 0:
                    pe.wait_ge(zt_v_in, 16 * 9 * i + 16 * 9)
                if u:
                    pe.wait_ge(misc_dve, MD_S + md_out(u - 1) + MD_PAIR * i)
                e = slice(h * HD, (h + 1) * HD)
                terms = ([(0, 0, n - 1)] if n else []) + [(0, 1, n), (1, 2, n), (1, 3, n)]
                for x, (s, blk, key) in enumerate(terms):
                    g = (0, 0, 1, 2)[blk]
                    ins = T.matmul(ps[:, 7, (u % 4) * P + s * HD:(u % 4) * P + (s + 1) * HD],
                                   probT[:, u % 2, blk * P:(blk + 1) * P], vt[b][:, g, key, e],
                                   start=blk in ((0 if n else 1), 2), stop=blk in (1, 3))
                ins.then_inc(o_done, 1)

            with pe.Fori(0, NPAIR // 2) as i2:
                for b in range(2):
                    i = i2 * 2 + b
                    pe.wait_ge(zt_qk_in, 16 * 10 * i + 16 * 10)
                    pe.wait_ge(misc_dve, MD_S + md_scores(7) - MD_PAIR + MD_PAIR * i)

                    def gate_bank_free(m):
                        if m % 2:
                            pe.wait_ge(dve_evac, DE_Z - 1 + m // 2)
                        pe.wait_ge(act_evac, AE_Z - 3 + m + 4 * i)
                    gates = columns(W_GATE + 4 * i, 4, by_feature, h_acts, gate_bank_free)
                    for s in range(6):
                        if s < 3:
                            pe.wait_ge(misc_act, MA_Y + (-3, -2, 0)[s] + MA_PAIR * i)
                        if s == 3:
                            pe.wait_ge(misc_dve, MD_S + MD_PAIR * i)
                        if s == 4:
                            for _ in range(4):
                                next(gates)
                            pe.wait_ge(zt_k_in, 16 * 8 * i + 16 * 8)
                        if s >= 4:
                            pe.wait_ge(misc_act, MA_Y + s - 3 + MA_PAIR * i)
                        for n in range(TB):
                            ins = T.transpose(ps[:, 4 + s % 4, n * P:(n + 1) * P], zt[:, s, n], ident[:, :])
                        ins.then_inc(qk_turned, 1)
                    next(gates)
                    pe.wait_ge(misc_act, MA_Y + 3 + MA_PAIR * i)
                    pe.wait_ge(misc_dve, MD_S + 3 + MD_PAIR * i)
                    for u in range(10):
                        if u < 8:
                            scores(i, u)
                        for _ in range((1, 1, 1, 2, 1, 1, 2, 1, 0, 1)[u]):
                            next(gates)
                        if 1 <= u < 9:
                            turn_prob(i, u - 1)
                        if u >= 2:
                            values(i, u - 2, b)
            def by_act(a0):
                return lambda m: pe.wait_ge(act_evac, a0 + m + 1)

            def by_dve(d0):
                return lambda m: pe.wait_ge(dve_evac, d0 + m + 1)

            pe.wait_ge(yT_lo_done, 4)
            w = W_MIX
            run(columns(w, 2, by_feature, y_acts, by_act(AE_G - 4)))
            run(columns(w + 2, 2, by_feature, y_acts, by_act(AE_G)))
            run(columns(w + 4, 2, by_feature, y_acts, by_dve(DE_Z)))
            glu = columns(w + 6, 2, by_feature, y_acts, by_act(AE_G + 4))
            for _ in range(4):
                next(glu)
            pe.wait_ge(a_ready, 1)
            pe.wait_ge(misc_act, MA_ATT)
            pe.wait_ge(misc_dve, MD_ATT)
            for k in range(4):
                for n in range(TB):
                    ins = T.transpose(ps[:, 4 + k, n * P:(n + 1) * P],
                                      a_tok[:, n, 2 * k:2 * k + 2].rearrange("p g e -> p (g e)"), ident[:, :])
                ins.then_inc(a_turned, 1)
            run(glu)
            for c in range(2):
                run(columns(w + 8 + 2 * c, 2, by_feature, a_acts, by_dve(DE_Z + 4 + 4 * c), split_rows(aT_lo_done, 0)))
            for c in range(2):
                run(columns(W_OUT + 4 * c, 4, by_token, h_acts, by_dve(DE_GLU + 4 + 4 * c), split_rows(mix_lo_done, 0)))
            pe.wait_ge(dve_evac, DE_OUT)
            rows_turned(1, xn2)

            with pe.Fori(0, FB) as f:
                for j in range(4):
                    w = W_FFN + j + 4 * f
                    pe.wait_ge(w_lo_done, w + 1)
                    for m in range(4):
                        if j == 0:
                            if m < 2:
                                pe.wait_ge(act_evac, AE_GLU - 1 + m + 2 * f)
                            else:
                                pe.wait_ge(s_raw_done, 2 * f + m - 1)
                        turned_rows(KT, j, m)
                        for h in range(2):
                            for k, (a, b) in enumerate(((0, 0), (1, 0), (0, 1))):
                                at_w = m // 2 * 512 + h * 256 + m % 2 * P
                                ins = T.matmul(ps[:, m], (w_hi, w_lo)[b][:, j % WSPL, at_w:at_w + P],
                                               h_acts[a][:, 2 * j + h, :], start=j == 0 and h == 0 and k == 0,
                                               stop=j == 3 and h == 1 and k == 2)
                        ins.then_inc(gemm_steps, 1)

            def down(w, j, row, first, last):
                pe.wait_ge(w_lo_done, w + 1)
                pe.wait_ge(s_lo_done, row + 1)
                for m in ((4, 5, 6, 7, 0, 1, 2, 3) if first else range(2 * TB)):
                    if first and m == 0:
                        pe.wait_ge(act_evac, AE_F)
                        pe.wait_ge(s_raw_done, 2 + 2 * FB)
                    n, h = m // 2, m % 2
                    for k, (a, b) in enumerate(((0, 0), (1, 0), (0, 1))):
                        ins = T.matmul(ps[:, m], y_acts[a][:, j % 2, n * P:(n + 1) * P],
                                       (w_hi, w_lo)[b][:, j % WSPL, h * 512:(h + 1) * 512], start=first and k == 0, stop=last and k == 2,
                                       skip_group_check=not (first or last))
                    if last:
                        ins.then_inc(down_done, 1)
                    elif m % 2:
                        ins.then_inc(gemm_steps, 1)

            down(W_DOWN, 0, 0, True, False)
            with pe.Fori(0, (FT - 2) // 4) as q:
                for j in range(1, 5):
                    down(W_DOWN + j + 4 * q, j, q * 4 + j, False, False)
            down(W_END - 1, 1, FT - 1, False, True)


def constants():
    q = np.arange(P)[:, None]
    k = np.arange(P)[None, :]
    tq, tk = 4 * (q % 32) + q // 32, 4 * (k % 32) + k // 32
    allowed = [k >= q, k <= q, tk <= tq, (q // 32 == k // 32) & (k <= q)]
    masks = np.concatenate([np.where(a, 0.0, NEG) for a in allowed], axis=1).astype(np.float32)
    return {"masks": masks, "ident": np.eye(P, dtype=np.float32),
            "eye16": (q % CH == np.arange(CH)[None, :]).astype(np.float32)}


def kernel(**inputs):
    import concourse.bacc as _bacc
    from concourse.bass_utils import run_bass_kernel_spmd as _run

    nc = _bacc.Bacc("TRN2", target_bir_lowering=False, num_devices=1)
    arrays, dram = {}, {}
    for name, a in {**inputs, **constants()}.items():
        a = np.ascontiguousarray(a)
        if name.startswith("w_"):
            a = a[0]
        arrays["in_" + name] = a
        dram[name] = nc.dram_tensor("in_" + name, a.shape, mybir.dt.from_np(a.dtype), kind="ExternalInput").ap()
    dram["out"] = nc.dram_tensor("out_0", (1, SEQ, DM), F32, kind="ExternalOutput").ap()
    build(nc, dram)
    r = _run(nc, [arrays], core_ids=[0])
    return r.results[0]["out_0"]
```
